# Optimizing a Trainium2 kernel written in Bass

```python
import math
import jax, jax.numpy as jnp
from jax import lax
import numpy as np

D_MODEL = 1024
BATCH = 1
SEQ = 1024
DEPTH = 1

ATT_HEADS = 6
ATT_HEAD_DIM = 64
ATT_WIDTH = ATT_HEADS * ATT_HEAD_DIM
IDX_HEADS = 4
IDX_DIM = 64
TOPK_MAX = 256
QBLOCK = 32
POOL_GROUPS = 4
POOL_GROUP_DIM = 64
POOL_WIDTH = POOL_GROUPS * POOL_GROUP_DIM
POOL_WINDOWS = (2, 4, 8, 16)
GLA_HEADS = 4
GLA_DK = 48
GLA_DV = 96
GLA_KEY_WIDTH = GLA_HEADS * GLA_DK
GLA_VAL_WIDTH = GLA_HEADS * GLA_DV
GLA_GATE_RANK = 16
GLA_TAU = 16.0
GLA_CHUNK = 64

MIX_WIDTH = ATT_WIDTH + POOL_WIDTH + GLA_VAL_WIDTH
EPS = 1e-6

IN_SPLITS = (
    ATT_WIDTH, ATT_WIDTH, ATT_WIDTH, ATT_WIDTH,
    IDX_HEADS * IDX_DIM, IDX_DIM, IDX_HEADS,
    POOL_WIDTH, POOL_WIDTH,
    GLA_KEY_WIDTH, GLA_KEY_WIDTH, GLA_VAL_WIDTH,
    GLA_GATE_RANK, GLA_VAL_WIDTH,
)
IN_WIDTH = sum(IN_SPLITS)

kernel_name = "hybrid_dsa_pool_gla_parallel"

def rms_norm(x, gain):
    xf = x.astype(jnp.float32)
    y = xf * lax.rsqrt(jnp.mean(xf * xf, axis=-1, keepdims=True) + EPS)
    return (y * gain.astype(jnp.float32)).astype(x.dtype)

def split_columns(p):
    offs = np.cumsum(IN_SPLITS)[:-1].tolist()
    return jnp.split(p, offs, axis=-1)

def sparse_attention(q, k, v, iq, ik, iw):
    B, S, H, D = q.shape
    topk = min(TOPK_MAX, S // 4)
    nb = S // QBLOCK

    def to_blocks(a):
        return jnp.swapaxes(a.reshape((B, nb, QBLOCK) + a.shape[2:]), 0, 1)

    ikf = ik.astype(jnp.float32)
    key_pos = jnp.arange(S)

    def one_block(args):
        qb, iqb, iwb, n = args
        tpos = n * QBLOCK + jnp.arange(QBLOCK)
        s = jax.nn.relu(jnp.einsum('bqhd,bsd->bqhs', iqb.astype(jnp.float32), ikf))
        score = jnp.einsum('bqhs,bqh->bqs', s, iwb.astype(jnp.float32))
        causal = key_pos[None, :] <= tpos[:, None]
        score = jnp.where(causal[None], score, -jnp.inf)
        _, idx = lax.top_k(score, topk)
        kg = jax.vmap(lambda kk, ii: kk[ii])(k, idx)
        vg = jax.vmap(lambda vv, ii: vv[ii])(v, idx)
        logits = jnp.einsum('bqhd,bqkhd->bhqk', qb, kg).astype(jnp.float32)
        valid = idx <= tpos[None, :, None]
        logits = jnp.where(valid[:, None], logits, -jnp.inf)
        p = jax.nn.softmax(logits, axis=-1)
        return jnp.einsum('bhqk,bqkhd->bqhd', p.astype(v.dtype), vg)

    out = lax.map(one_block, (to_blocks(q), to_blocks(iq), to_blocks(iw),
                              jnp.arange(nb, dtype=jnp.int32)))
    return jnp.swapaxes(out, 0, 1).reshape(B, S, H, D)

def pool_mixer(u, w_pool, scale):
    B, S, _ = u.shape
    ug = u.astype(jnp.float32).reshape(B, S, POOL_GROUPS, POOL_GROUP_DIM)
    c = jnp.concatenate([jnp.zeros((B, 1, POOL_GROUPS, POOL_GROUP_DIM), jnp.float32),
                         jnp.cumsum(ug, axis=1)], axis=1)
    t = jnp.arange(S)
    pooled = []
    for g, w in enumerate(POOL_WINDOWS):
        start = jnp.maximum(t + 1 - w, 0)
        count = jnp.minimum(t + 1, w).astype(jnp.float32)
        mean = (c[:, t + 1, g] - c[:, start, g]) / count[None, :, None]
        pooled.append(mean - ug[:, :, g])
    pooled = jnp.stack(pooled, axis=2)
    y = jnp.einsum('bsgc,gcd->bsgd', pooled, w_pool.astype(jnp.float32))
    y = y * scale.astype(jnp.float32).reshape(POOL_GROUPS, POOL_GROUP_DIM)
    return y.reshape(B, S, POOL_WIDTH).astype(u.dtype)

def gla_chunked(q, k, v, glog):
    B, S, H, DK = q.shape
    DV = v.shape[-1]
    C = GLA_CHUNK
    N = S // C

    def to_chunks(a):
        return a.astype(jnp.float32).reshape(B, N, C, H, a.shape[-1]).transpose(1, 0, 3, 2, 4)

    qc, kc, vc, gc = to_chunks(q), to_chunks(k), to_chunks(v), to_chunks(glog)
    b = jnp.cumsum(gc, axis=-2)
    qt = qc * jnp.exp(b) * (DK ** -0.5)
    kt = kc * jnp.exp(-b)
    kd = kc * jnp.exp(b[..., -1:, :] - b)
    decay_end = jnp.exp(b[..., -1, :])
    tri = jnp.tril(jnp.ones((C, C), dtype=bool))
    a_intra = jnp.where(tri, jnp.einsum('nbhid,nbhjd->nbhij', qt, kt), 0.0)
    o_intra = jnp.einsum('nbhij,nbhje->nbhie', a_intra, vc)

    def step(state, inp):
        qt_n, kd_n, v_n, dec_n = inp
        o = jnp.einsum('bhid,bhde->bhie', qt_n, state)
        state = dec_n[..., None] * state + jnp.einsum('bhjd,bhje->bhde', kd_n, v_n)
        return state, o

    state0 = jnp.zeros((B, H, DK, DV), jnp.float32)
    _, o_inter = lax.scan(step, state0, (qt, kd, vc, decay_end))
    o = (o_intra + o_inter).transpose(1, 0, 3, 2, 4).reshape(B, S, H, DV)
    return o.astype(v.dtype)

def hybrid_layer(x, norm_g, w_in, att_q_gain, att_k_gain, pool_w, pool_scale,
                 gla_w_gate, gla_b_gate, gla_out_gain, w_out):
    B, S, _ = x.shape
    h = rms_norm(x, norm_g)
    proj = h @ w_in
    (aq, ak, av, az, iq, ik, iw, pu, pz, gq, gk, gv, gg, gz) = split_columns(proj)

    q = rms_norm(aq.reshape(B, S, ATT_HEADS, ATT_HEAD_DIM), att_q_gain) * (ATT_HEAD_DIM ** -0.5)
    k = rms_norm(ak.reshape(B, S, ATT_HEADS, ATT_HEAD_DIM), att_k_gain)
    v = av.reshape(B, S, ATT_HEADS, ATT_HEAD_DIM)
    iq = iq.reshape(B, S, IDX_HEADS, IDX_DIM)
    iw = iw * (IDX_HEADS ** -0.5)
    ya = sparse_attention(q, k, v, iq, ik, iw).reshape(B, S, ATT_WIDTH) * jax.nn.silu(az)

    yb = pool_mixer(pu, pool_w, pool_scale) * jax.nn.silu(pz)

    glog = jax.nn.log_sigmoid((gg @ gla_w_gate + gla_b_gate).astype(jnp.float32)) / GLA_TAU
    glog = glog.reshape(B, S, GLA_HEADS, GLA_DK)
    yc = gla_chunked(gq.reshape(B, S, GLA_HEADS, GLA_DK), gk.reshape(B, S, GLA_HEADS, GLA_DK),
                     gv.reshape(B, S, GLA_HEADS, GLA_DV), glog)
    yc = rms_norm(yc, gla_out_gain).reshape(B, S, GLA_VAL_WIDTH) * jax.nn.silu(gz)

    y = jnp.concatenate([ya, yb, yc], axis=-1) @ w_out
    return x + y

def setup_inputs(seed: int = 0) -> dict:
    key = jax.random.key(seed)
    ks = jax.random.split(key, 12)
    f32 = jnp.float32
    x = jax.random.normal(ks[0], (BATCH, SEQ, D_MODEL), f32)
    norm_g = 1.0 + 0.05 * jax.random.normal(ks[1], (DEPTH, D_MODEL), f32)
    w_in = jax.random.normal(ks[2], (DEPTH, D_MODEL, IN_WIDTH), f32) * D_MODEL ** -0.5
    att_q_gain = 1.0 + 0.05 * jax.random.normal(ks[3], (DEPTH, ATT_HEAD_DIM), f32)
    att_k_gain = 1.0 + 0.05 * jax.random.normal(ks[4], (DEPTH, ATT_HEAD_DIM), f32)
    pool_w = jax.random.normal(ks[5], (DEPTH, POOL_GROUPS, POOL_GROUP_DIM, POOL_GROUP_DIM), f32) * POOL_GROUP_DIM ** -0.5
    pool_scale = 1.0 + 0.1 * jax.random.normal(ks[6], (DEPTH, POOL_WIDTH), f32)
    gla_w_gate = jax.random.normal(ks[7], (DEPTH, GLA_GATE_RANK, GLA_KEY_WIDTH), f32) * GLA_GATE_RANK ** -0.5
    gla_b_gate = 0.1 * jax.random.normal(ks[8], (DEPTH, GLA_KEY_WIDTH), f32)
    gla_out_gain = 1.0 + 0.05 * jax.random.normal(ks[9], (DEPTH, GLA_DV), f32)
    w_out = jax.random.normal(ks[10], (DEPTH, MIX_WIDTH, D_MODEL), f32) * MIX_WIDTH ** -0.5
    return {"x": x, "norm_g": norm_g, "w_in": w_in, "att_q_gain": att_q_gain,
            "att_k_gain": att_k_gain, "pool_w": pool_w, "pool_scale": pool_scale,
            "gla_w_gate": gla_w_gate, "gla_b_gate": gla_b_gate,
            "gla_out_gain": gla_out_gain, "w_out": w_out}

def reference(x, norm_g, w_in, att_q_gain, att_k_gain, pool_w, pool_scale,
              gla_w_gate, gla_b_gate, gla_out_gain, w_out):
    for l in range(DEPTH):
        x = hybrid_layer(x, norm_g[l], w_in[l], att_q_gain[l], att_k_gain[l], pool_w[l],
                         pool_scale[l], gla_w_gate[l], gla_b_gate[l], gla_out_gain[l], w_out[l])
    return x


_drawn_inputs = setup_inputs


def setup_inputs(seed=0):
    import zlib

    import numpy as np

    out = dict(_drawn_inputs(seed))
    spreads = {}
    factors = {'att_q_gain': 8.0,
     'att_k_gain': 8.0,
     'gla_b_gate': 3.658,
     'gla_out_gain': 3.138,
     'pool_scale': 3.318}
    for name, (base, spread) in spreads.items():
        noise = np.random.default_rng([zlib.crc32(name.encode()), seed]).standard_normal(out[name].shape)
        drawn = base * np.exp(spread * noise) if base else spread * noise
        out[name] = __import__('jax').numpy.asarray(drawn.astype(out[name].dtype))
    for name, factor in factors.items():
        out[name] = (out[name] * factor).astype(out[name].dtype)
    return out
```

```python
from contextlib import ExitStack

import numpy as np
import concourse.bass as bass
from concourse import mybir

F32 = mybir.dt.float32
F32R = mybir.dt.float32r
BF16 = mybir.dt.bfloat16
U32 = mybir.dt.uint32
I32 = mybir.dt.int32
U8 = mybir.dt.uint8
ALU = mybir.AluOpType
ACT = mybir.ActivationFunctionType
AX = mybir.AxisListType

P = 128
S = 1024
D = 1024
T = S // P
K = D // P
EPS = 1e-6
HEADS, HD = 6, 64
PAIRS = HEADS // 2
IH, IDIM = 4, 64
TOPK = 256
T0 = TOPK // P
TS = T - T0
GH, GK, GV, RANK = 4, 48, 96, 16
GP = 64
TAU = 16.0
CH = 64
WB = 384
NEG = -3.0e38
NEGM = -1.0e30

IDXW = IH * IDIM + IDIM + IH + RANK
C0 = IDXW
CW = 3 * WB
A0 = C0 + CW
AW = 4 * WB
B0 = A0 + AW
BW = 512
WCOLS = B0 + 2 * WB
BLOCK_AT = [0] + [C0 + WB * i for i in range(3)] + [A0 + WB * i for i in range(6)]
BLOCK_W = [IDXW] + [WB] * 8 + [BW - WB]
NBLK = len(BLOCK_W)
NC_UNITS = 3 * T
MOFF = [P * t * (t + 1) // 2 for t in range(T + 1)]
SOFF = [MOFF[t] - MOFF[T0] for t in range(T + 1)]
PADL = 16

CI, CC, CTI, CTS, CON, CCH, CNT, CW1 = 0, 128, 256, 384, 512, 640, 642, 674
CONSTS = 676


class Chain:

    def __init__(self, engine, sem, after_loop_wait=None):
        self.engine, self.sem, self.n, self.off = engine, sem, 0, 0
        self.after_loop_wait = after_loop_wait

    def step(self, ins):
        ins.then_inc(self.sem, 1)
        self.n += 1

    def wait(self):
        self.engine.wait_ge(self.sem, self.off + self.n)
        if self.after_loop_wait and not isinstance(self.off, int):
            self.after_loop_wait(self.engine)

    def link(self, ins):
        self.step(ins)
        self.wait()

    def loop(self, i, stride):
        self.off, self.began, self.stride = i * stride, self.n, stride

    def end(self, rounds):
        assert self.n - self.began == self.stride, (self.n - self.began, self.stride)
        self.off = 0
        self.n += self.stride * (rounds - 1)


def program(nc, d):
    ctx = ExitStack()
    with ctx:
        def sb(name, shape, dt=F32):
            return ctx.enter_context(nc.sbuf_tensor(name, shape, dt))

        def sem(name):
            return ctx.enter_context(nc.semaphore(name))

        const = sb("const", [P, CONSTS])
        ident = const[:, CI:CI + P]
        causal = const[:, CC:CC + P]
        tri_upto = const[:, CTI:CTI + P]
        tri_after = const[:, CTS:CTS + P]
        ones = const[:, CON:CON + P]
        in_chunk = const[:, CCH:CCH + 2]
        pool_cnt = const[:, CNT:CNT + 32].rearrange("p (m t) -> p m t", m=2)
        pool_w1 = const[:, CW1:CW1 + 2]
        norm_g = sb("norm_g", [P, K])
        mask = sb("mask", [P, MOFF[T]], BF16)
        iw = sb("iw", [P, T, IH])
        gg = sb("gg", [P, T, RANK])
        ssx = sb("ssx", [P, T])
        rstd = sb("rstd", [P, T])
        rtmp = sb("rtmp", [P, 32])
        neghalf = sb("neghalf", [P, 32])
        qgain = sb("qgain", [P, HD])
        kgain = sb("kgain", [P, HD])
        gain_o = sb("gain_o", [P, GV])
        wg = sb("wg", [RANK + 1, GH * GK])
        pscale = sb("pscale", [P, 2])
        cnt = sb("cnt", [P, TS])
        pat = sb("pat", [P, TS], U32)
        cand = sb("cand", [P, TS], U32)
        inc = sb("inc", [P, TS], U32)
        bit = sb("bit", [P, TS], U32)
        need = sb("need", [P, TS])
        gss = sb("gss", [P, GH])
        grs = sb("grs", [P, GH])
        gdec = sb("gdec", [P, 4])
        dec = sb("dec", [P, 2, 4])
        mx = sb("mx", [P, 2])
        nmx = sb("nmx", [P, 2])
        rsum = sb("rsum", [P, T, 2])
        rinv = sb("rinv", [P, T, 2])
        ssq = sb("ssq", [P, 32])
        rqk = sb("rqk", [P, 32])

        kib = 1024
        placed = {}

        def place(items):
            with ExitStack() as layer:
                at = 0
                for name, shape, dt, first in sorted(items, key=lambda x: x[3]):
                    assert first >= at, (name, first, at)
                    if first > at:
                        layer.enter_context(nc.sbuf_tensor(f"gap_{name}", [P, first - at], U8))
                    placed[name] = layer.enter_context(nc.sbuf_tensor(name, shape, dt))
                    size = int(np.prod(shape[1:])) * {F32: 4, F32R: 4, BF16: 2, U8: 1}[dt]
                    at = first + (size + 31) // 32 * 32
                    placed.setdefault("top", 0)
                    placed["top"] = max(placed["top"], at)

        SC, RL, EV, GL = 124 * kib, 141 * kib, 150 * kib, 156 * kib
        place([("hT_hi", [P, K, S], F32R, 0), ("hT_lo", [P, K, S], F32R, 32 * kib),
               ("w_hi", [P, 2, K, WB], F32R, 64 * kib), ("w_lo", [P, 2, K, WB], F32R, 88 * kib),
               ("w_raw", [P, K, WB], F32, 112 * kib),
               ("scores", [P, SOFF[T]], F32, SC), ("relus", [P, 2, S], F32, RL),
               ("evac", [P, 4, WB], F32, EV),
               ("stage", [P, 2, 6, P], F32, GL), ("iqT", [P, IH, TS * P], F32R, GL + 6 * kib),
               ("ikT", [P, 2, S], F32R, GL + 18 * kib)])
        g = GL
        gla = []
        for name, shape, dt in (
                ("gin", [P, 2, CW], F32), ("ggs", [P, RANK], F32), ("ggT", [RANK + 1, P], F32), ("nl", [P, GH, GP], F32),
                ("sp_a", [P, GH, GK], F32), ("sp_r", [P, GH, GK], F32), ("eb", [P, GH, GK], F32),
                ("enb", [P, GH, GK], F32), ("ed", [P, GH, GK], F32), ("qs", [P, GH, GP], F32),
                ("ks", [P, GH, GP], F32), ("kd", [P, GH, GP], F32), ("qkT", [P, 2, 4, P], F32),
                ("kv", [P, 2, 2, 2, GV], F32), ("state", [P, 5, 2, GV], F32),
                ("att", [P, GH, P], F32), ("osb", [P, GH, GV], F32), ("osq", [P, GH, GV], F32),
                ("yT", [P, 3, P], F32)):
            gla.append((name, shape, dt, g))
            g += int(np.prod(shape[1:])) * 4
        place(gla)
        place([("xT_raw", [P, 4, S], F32, SC), ("x_ring", [P, 2, D], F32, RL)])
        place([("uT", [P, 2, PADL + S], F32, SC), ("zT", [P, 2, S], F32, SC + 8320),
               ("win", [P, 2, PADL + S], F32, RL)])
        place([("rdiag", [P, T, P], F32, RL), ("rstdB", [P, S], F32, EV), ("wpd", [P, 2, P], F32, EV + 4 * kib)])
        place([("wo_hi", [P, K, 512], F32R, 0), ("wo_lo", [P, K, 512], F32R, 16 * kib),
               ("wo_raw", [P, 4, 512], F32, 32 * kib), ("mixA", [P, PAIRS, S], F32, 40 * kib),
               ("qT", [P, 2, S], F32R, 52 * kib), ("kT", [P, 2, 2, S], F32R, 60 * kib),
               ("prob", [P, 2, S], F32, 76 * kib), ("probT", [P, 2, T, P], F32, 84 * kib),
               ("oT", [P, S], F32, 92 * kib), ("v", [P, T, P], F32, 96 * kib),
               ("gate", [P, T, P], F32, 100 * kib),
               ("raw_qk", [P, 2, T, P], F32, GL), ("sq", [P, 2, T, P], F32, GL + 8 * kib),
               ("qk_st", [P, 2, 2, T, P], F32, GL + 16 * kib)])
        place([("mix_hi", [P, K, S], F32R, 52 * kib), ("mix_lo", [P, K, S], F32R, 84 * kib),
               ("res", [P, 4, 512], F32, SC), ("outb", [P, 4, 512], F32, SC + 8 * kib),
               ("mix_raw", [P, 2, S], F32, RL),
               ("wo_hi2", [P, K, 512], F32R, GL), ("wo_lo2", [P, K, 512], F32R, GL + 16 * kib)])
        v_ = placed
        hT_hi, hT_lo, w_hi, w_lo, w_raw = (v_[n] for n in ("hT_hi", "hT_lo", "w_hi", "w_lo", "w_raw"))
        scores, relus, evac, stage, iqT, ikT = (v_[n] for n in ("scores", "relus", "evac", "stage", "iqT", "ikT"))
        (gin, ggs, ggT, nl, sp_a, sp_r, eb, enb, ed, qs, ks, kd, qkT, kv, state, att, osb, osq, yT) = (
            v_[n[0]] for n in gla)
        xT_raw, x_ring, uT, zT, win, rdiag, rstdB, wpd = (
            v_[n] for n in ("xT_raw", "x_ring", "uT", "zT", "win", "rdiag", "rstdB", "wpd"))
        (wo_hi, wo_lo, wo_raw, mixA, qT, kT, prob, probT, oT, v, gate, raw_qk, sq, qk_st, mix_hi, mix_lo, res,
         outb, mix_raw, wo_hi2, wo_lo2) = (v_[n] for n in (
             "wo_hi", "wo_lo", "wo_raw", "mixA", "qT", "kT", "prob", "probT", "oT", "v", "gate", "raw_qk", "sq",
             "qk_st", "mix_hi", "mix_lo", "res", "outb", "mix_raw", "wo_hi2", "wo_lo2"))
        relu_flat = relus[:, :, :].rearrange("p a n -> p (a n)")
        seen = relu_flat.bitcast(U8)
        whole = ctx.enter_context(nc.sbuf_tensor("region", [P, v_["top"]], U8))
        del whole

        pA = ctx.enter_context(nc.psum_tensor("pA", [P, 2, 512], F32))
        pB = ctx.enter_context(nc.psum_tensor("pB", [P, 2, 512], F32))
        p4, p5, p6, p7 = (ctx.enter_context(nc.psum_tensor(f"p{i}", [P, 512], F32)) for i in range(4, 8))
        bank = [pA[:, 0, :], pA[:, 1, :], pB[:, 0, :], pB[:, 1, :], p4[:, :], p5[:, :], p6[:, :], p7[:, :]]

        proj_c = nc.dram_tensor("proj_c", [S, CW], F32).ap()
        proj_a = nc.dram_tensor("proj_a", [S, AW], F32).ap()
        mix_d = nc.dram_tensor("mix_d", [K - PAIRS, P, S], F32).ap()

        const_in = sem("const_in")
        xT_in = [sem(f"xT_in{i}") for i in range(4)]
        x_in = [sem(f"x_in{i}") for i in range(2)]
        w_in = [sem(f"w_in{k}") for k in range(K)]
        hT_ready, w_ready = sem("hT_ready"), sem("w_ready")
        x_squared, rstd_ready = sem("x_squared"), sem("rstd_ready")
        idx_made, idx_staged, idx_turned, idx_kept = (
            sem("idx_made"), sem("idx_staged"), sem("idx_turned"), sem("idx_kept"))
        dots_made, dots_relu, dots_added = sem("dots_made"), sem("dots_relu"), sem("dots_added")
        proj_made, proj_kept = sem("proj_made"), sem("proj_kept")
        spilled = [sem(f"spilled{i}") for i in range(4)]
        mask_ready = sem("mask_ready")
        dve_done, act_done, pool_done = sem("dve_done"), sem("act_done"), sem("pool_done")
        gin_in = [sem(f"gin_in{i}") for i in range(2)]
        ggs_ready = sem("ggs_ready")
        ggT_made, z_made, sums_made, qkT_made, att_made, o_made, y_turned = (
            sem(n) for n in ("ggT_made", "z_made", "sums_made", "qkT_made", "att_made", "o_made", "y_turned"))
        ggT_kept, sp_kept, exps_kept, qkT_kept, att_kept, o_kept, y_kept = (
            sem(n) for n in ("ggT_kept", "sp_kept", "exps_kept", "qkT_kept", "att_kept", "o_kept", "y_kept"))
        nl_done, scaled_done, state_done, masked_done, y_done = (
            sem(n) for n in ("nl_done", "scaled_done", "state_done", "masked_done", "y_done"))
        kv_kept, y_out, gla_clear = sem("kv_kept"), sem("y_out"), sem("gla_clear")
        rdiag_ready, rstdB_made, rstdB_ready = sem("rdiag_ready"), sem("rstdB_made"), sem("rstdB_ready")
        wpd_clear, wpd_in = sem("wpd_clear"), sem("wpd_in")
        pf_made, pf_kept, silu_done = sem("pf_made"), sem("pf_kept"), sem("silu_done")
        pooled_done, yb_made, yb_done, yb_out = sem("pooled_done"), sem("yb_made"), sem("yb_done"), sem("yb_out")
        qk_in, v_in, z_in = sem("qk_in"), sem("v_in"), sem("z_in")
        qk_squared, qk_summed, qk_split = sem("qk_squared"), sem("qk_summed"), sem("qk_split")
        tb_made, tb_kept = [sem(f"tb_made{i}") for i in range(2)], [sem(f"tb_kept{i}") for i in range(2)]
        logits_made, logits_read, max_ready, prob_done = (
            sem(n) for n in ("logits_made", "logits_read", "max_ready", "prob_done"))
        pv_made, pv_kept, gate_silu, gate_done, mixA_done = (
            sem(n) for n in ("pv_made", "pv_kept", "gate_silu", "gate_done", "mixA_done"))
        passed = sem("passed")
        wo_in = [sem(f"wo_in{i}") for i in range(4)]
        wo_ready = sem("wo_ready")
        mix_in = [sem(f"mix_in{i}") for i in range(2)]
        mixhi_ready, mixlo_ready, out_made, out_added = (
            sem("mixhi_ready"), sem("mixlo_ready"), sem("out_made"), sem("out_added"))
        res_in = [sem(f"res_in{i}") for i in range(4)]
        out_out = [sem(f"out_out{i}") for i in range(4)]

        block = ctx.enter_context(nc.Block())
        SMALL = 8 * 16
        NU = NC_UNITS + 4 * T
        NDOT = TS * IH
        NBK = NU // 4 * 16
        OUT_ORDER = [3, 4, 5, 6, 7, 0, 1, 2]

        def flat(ap):
            return ap.rearrange("p a n -> p (a n)")

        def tiles(t0, n=1):
            return slice(t0 * P, (t0 + n) * P)

        def idx_kept_after(t):
            return t + 1 if t < T0 else T0 + 2 * (t + 1 - T0)

        def groups(t):
            return [range(a, min(a + 4, t + 1)) for a in range(0, t + 1, 4)]

        def turned_at(s):
            before = sum(len(groups(n % T)) for n in range(s))
            return [(g % 2, 4 + g // 2 + 1) for g in range(before, before + len(groups(s % T)))]

        NG = 4 + sum(len(groups(s % T)) for s in range(2 * T)) // 2 + 1

        def alone(engine):
            engine.sem_inc(passed, 1)

        @block.sync
        def _(sp):
            def load_w(n_at, width, k):
                return sp.dma_start(w_raw[:, k, 0:width], d["w"][k * P:(k + 1) * P, n_at:n_at + width])

            sp.dma_start(norm_g[:, :], d["norm_g"]).then_inc(const_in, 16)
            for k in range(K):
                if k >= 4:
                    sp.wait_ge(hT_ready, k - 3)
                sp.dma_start(xT_raw[:, k % 4, :], d["xT"][k * P:(k + 1) * P, :]).then_inc(xT_in[k % 4], 16)
                load_w(0, BLOCK_W[0], k).then_inc(w_in[k], 16)
            for name, dst in (("const", const[:, :]), ("qgain", qgain[:, :]), ("kgain", kgain[:, :]),
                              ("gain_o", gain_o[:, :]), ("pscale", pscale[:, :]),
                              ("w_gate", wg[0:RANK, :]), ("b_gate", wg[RANK:RANK + 1, :])):
                sp.dma_start(dst, d[name]).then_inc(const_in, 16)
            for t in range(T):
                if t >= 2:
                    sp.wait_ge(x_squared, t - 1)
                sp.dma_start(x_ring[:, t % 2, :], d["x"][tiles(t), :]).then_inc(x_in[t % 2], 16)
                sp.wait_ge(w_ready, t + 1)
                load_w(BLOCK_AT[1], WB, t).then_inc(w_in[t], 16)
            for k in range(K):
                sp.wait_ge(w_ready, K + k + 1)
                load_w(BLOCK_AT[2], WB, k).then_inc(w_in[k], 16)
            for n in range(1, 4):
                for t in range(T):
                    u = (n - 1) * T + t
                    sp.wait_ge(proj_kept, u + 1)
                    sp.dma_start(proj_c[tiles(t), (n - 1) * WB:n * WB], evac[:, u % 4, :]).then_inc(spilled[u % 4], 16)
                    sp.wait_ge(w_ready, K * (n + 1) + t + 1)
                    load_w(BLOCK_AT[n + 2], WB, t).then_inc(w_in[t], 16)
            for i in range(4):
                sp.wait_ge(spilled[i], NC_UNITS // 4 * 16)
            with sp.Fori(0, 2) as it:
                for b in range(2):
                    blk = it * 2 + b
                    for j in range(2):
                        sp.wait_ge(y_done, it * 4 + (2 * b + j) + 1)
                        sp.dma_start(gin[:, j, :], proj_c[bass.ds((blk * 2 + j) * P, P), :]).then_inc(gin_in[j], 16)
                    for t in range(T):
                        sp.wait_ge(proj_kept, it * 16 + (NC_UNITS + 8 * b + t + 1))
                        sp.dma_start(proj_a[tiles(t), bass.ds(blk * WB, WB)], evac[:, t % 4, :]).then_inc(spilled[t % 4], 16)
                        sp.wait_ge(w_ready, it * 16 + (K * (5 + b) + t + 1))
                        sp.dma_start(w_raw[:, t, :], d["w"][t * P:(t + 1) * P, bass.ds(blk * WB + (A0 + 2 * WB), WB)]).then_inc(w_in[t], 16)
                        if t >= 6:
                            j = t - 6
                            sp.wait_ge(y_kept, it * 4 + (2 * b + j) + 2)
                            sp.dma_start(mix_d[2:5, :, bass.ds((blk * 2 + j) * P, P)].rearrange("c p n -> p c n"),
                                         yT[:, :, :]).then_inc(y_out, 16)
            for i in range(4):
                sp.wait_ge(spilled[i], NBK)
            sp.wait_ge(y_kept, T + 1)
            for w in range(2):
                sp.dma_start(raw_qk[:, w, :, :], proj_a[:, w * WB:w * WB + P].rearrange("(t p) n -> p t n", p=P)).then_inc(qk_in, 16)
            sp.wait_ge(wpd_clear, 1)
            for grp in range(4):
                o = HD * (grp % 2)
                sp.dma_start(wpd[o:o + HD, grp // 2, o:o + HD], d["pool_w"][grp]).then_inc(wpd_in, 16)
            sp.wait_ge(pf_made, 8)
            sp.dma_start(v[:, :, :], proj_a[:, 2 * WB:2 * WB + P].rearrange("(t p) n -> p t n", p=P)).then_inc(v_in, 16)
            sp.dma_start(gate[:, :, :], proj_a[:, 3 * WB:3 * WB + P].rearrange("(t p) n -> p t n", p=P)).then_inc(z_in, 16)
            for k in range(4):
                sp.dma_start(wo_raw[:, k, :], d["w_out"][OUT_ORDER[k] * P:(OUT_ORDER[k] + 1) * P, 0:512]).then_inc(wo_in[k], 16)
            for u in range(4):
                sp.wait_ge(yb_done, u + 1)
                sp.dma_start(mix_d[u // 2, :, 512 * (u % 2):512 * (u % 2) + 512], zT[:, u // 2, 512 * (u % 2):512 * (u % 2) + 512]).then_inc(yb_out, 16)
            for k in range(4, K):
                sp.wait_ge(wo_ready, k - 3)
                sp.dma_start(wo_raw[:, k % 4, :], d["w_out"][OUT_ORDER[k] * P:(OUT_ORDER[k] + 1) * P, 0:512]).then_inc(wo_in[k % 4], 16)
            with sp.Fori(0, PAIRS - 1) as p:
                sp.wait_ge(qk_split, p + 1)
                for w in range(2):
                    sp.dma_start(raw_qk[:, w, :, :], proj_a[:, bass.ds(p * P + (w * WB + P), P)].rearrange("(t p) n -> p t n", p=P)).then_inc(qk_in, 16)
                sp.wait_ge(pv_made, p * 16 + 18)
                sp.dma_start(v[:, :, :], proj_a[:, bass.ds(p * P + (2 * WB + P), P)].rearrange("(t p) n -> p t n", p=P)).then_inc(v_in, 16)
                for g in range(2):
                    sp.wait_ge(tb_made[g], p * NG + NG)
                sp.dma_start(gate[:, :, :], proj_a[:, bass.ds(p * P + (3 * WB + P), P)].rearrange("(t p) n -> p t n", p=P)).then_inc(z_in, 16)
            sp.wait_ge(yb_out, 4 * 16)
            sp.wait_ge(y_out, (T + 1) * 16)
            for n in range(2):
                sp.dma_start(mix_raw[:, n, :], mix_d[n]).then_inc(mix_in[n], 16)
            for t in range(4):
                sp.dma_start(res[:, t, :], d["x"][tiles(t), 0:512]).then_inc(res_in[t], 16)
            for k in range(K):
                if k < 3:
                    sp.wait_ge(mixlo_ready, k + 1)
                    sp.wait_ge(mixhi_ready, k + 1)
                    sp.dma_start(mix_raw[:, k % 2, :], mix_d[k + 2]).then_inc(mix_in[k % 2], 16)
                sp.wait_ge(wo_ready, K + k - 3)
                sp.dma_start(wo_raw[:, k % 4, :], d["w_out"][OUT_ORDER[k] * P:(OUT_ORDER[k] + 1) * P, 512:1024]).then_inc(wo_in[k % 4], 16)
            for u in range(2 * T):
                t, half = u % T, u // T
                sp.wait_ge(out_added, u + 1)
                sp.dma_start(d["out"][tiles(t), 512 * half:512 * half + 512], outb[:, u % 4, :]).then_inc(out_out[u % 4], 16)
                if u + 4 < 2 * T:
                    t, half = (u + 4) % T, (u + 4) // T
                    sp.dma_start(res[:, u % 4, :], d["x"][tiles(t), 512 * half:512 * half + 512]).then_inc(res_in[u % 4], 16)
            for i in range(4):
                sp.wait_ge(out_out[i], 4 * 16)

        @block.tensor
        def _(pe):
            def project(out, t, buf, width, first_k=0, last_k=K, ready=None):
                for k in range(first_k, last_k):
                    if ready is not None:
                        pe.wait_ge(w_ready, ready + k + 1)
                    for n, (a, w) in enumerate(((hT_hi, w_hi), (hT_hi, w_lo), (hT_lo, w_hi))):
                        last = nc.tensor.matmul(out, a[:, k, tiles(t)], w[:, buf, k, 0:width],
                                                start=(k == 0 and n == 0), stop=(k == K - 1 and n == 2))
                return last

            for k in range(K):
                pe.wait_ge(hT_ready, k + 1)
                pe.wait_ge(w_ready, k + 1)
                for t in range(T):
                    last = project(bank[t][:, 0:IDXW], t, 0, IDXW, k, k + 1)
                    if k == K - 1:
                        last.then_inc(idx_made, 1)
            pe.wait_ge(const_in, SMALL)
            for t in range(T):
                pe.wait_ge(idx_staged, t + 1)
                if t >= T0:
                    for h in range(IH):
                        nc.tensor.transpose(bank[t][:, h * P:(h + 1) * P], stage[:, t % 2, h, :], ident)
                    pe.wait_ge(idx_kept, idx_kept_after(t - T0))
                for m in range(2):
                    last = nc.tensor.transpose(bank[t if t < T0 else t - T0][:, m * P:(m + 1) * P], stage[:, t % 2, 4 + m, :], ident)
                last.then_inc(idx_turned, 1)
            pe.wait_ge(idx_kept, idx_kept_after(T - 1))

            def dots(n):
                t, h = T0 + n // IH, n % IH
                width = (t + 1) * P
                if n >= 2:
                    pe.wait_ge(dots_relu, n - 1)
                dst = (pA, pB)[n % 2]
                for c in range(0, width, 512):
                    w = min(512, width - c)
                    for m in range(2):
                        last = nc.tensor.matmul(dst[:, c // 512, 0:w], iqT[:, h, (t - T0) * P:(t - T0 + 1) * P],
                                                ikT[:, m, c:c + w], start=(m == 0), stop=(m == 1))
                last.then_inc(dots_made, 1)

            for n in range(1, 4):
                for t in range(T):
                    u = (n - 1) * T + t
                    if n == 1 and t < TS:
                        for h in range(IH):
                            dots(t * IH + h)
                    if u >= 2:
                        pe.wait_ge(proj_kept, u - 1)
                    project(bank[4 + u % 2][:, 0:WB], t, n % 2, WB, ready=n * K if t == 0 else None).then_inc(proj_made, 1)

            pe.wait_ge(dots_relu, NDOT)
            pe.wait_ge(gla_clear, 1)

            def gla(stage_no, i, j, rounds):
                if stage_no == 1:
                    if j == 0:
                        pe.wait_ge(y_kept, i + 1)
                    pe.wait_ge(ggs_ready, i + 1)
                    nc.tensor.transpose(bank[0][0:RANK, 0:P], ggs[:, :], ident).then_inc(ggT_made, 1)
                if stage_no == 2:
                    pe.wait_ge(ggT_kept, i + 1)
                    nc.tensor.matmul(bank[1][:, 0:GH * GK], ggT[:, :], wg[:, :], start=True, stop=True).then_inc(z_made, 1)
                if stage_no == 3:
                    pe.wait_ge(nl_done, i + 1)
                    if j == 0:
                        pe.wait_ge(ggT_kept, i + 2)
                    nc.tensor.matmul(bank[2][:, 0:256], tri_upto, flat(nl[:, :, :]), start=True, stop=True)
                    nc.tensor.matmul(bank[2][:, 256:512], tri_after, flat(nl[:, :, :]), start=True, stop=True)
                    for p in range(2):
                        last = nc.tensor.matmul(bank[0][:, 2 * p:2 * p + 2], flat(nl[:, 2 * p:2 * p + 2, :]), in_chunk,
                                                start=True, stop=True)
                    last.then_inc(sums_made, 1)
                if stage_no == 4:
                    pe.wait_ge(scaled_done, i + 1)
                    pe.wait_ge(gin_in[j], rounds * 16 + 16)
                    if j == 1:
                        pe.wait_ge(kv_kept, i)
                    for n, src in enumerate((qs, ks)):
                        for p in range(2):
                            nc.tensor.transpose(bank[3][:, (2 * n + p) * P:(2 * n + p + 1) * P], flat(src[:, 2 * p:2 * p + 2, :]), ident)
                    for c in range(2):
                        rows = slice(CH * c, CH * c + CH)
                        for h in range(GH):
                            p, hh = h // 2, h % 2
                            last = nc.tensor.matmul(bank[6 + c][GP * hh:GP * hh + GP, GV * p:GV * p + GV], kd[rows, h, :],
                                                    gin[rows, j, WB + GV * h:WB + GV * h + GV], start=True, stop=True)
                    last.then_inc(qkT_made, 1)
                if stage_no == 5:
                    pe.wait_ge(qkT_kept, i + 1)
                    if j == 0:
                        pe.wait_ge(exps_kept, i + 2)
                    for h in (0, 2, 1, 3):
                        p, hh = h // 2, h % 2
                        rows = slice(GP * hh, GP * hh + GK)
                        last = nc.tensor.matmul(bank[2 - hh][:, p * P:(p + 1) * P], qkT[rows, j, 2 + p, :], qkT[rows, j, p, :],
                                                start=True, stop=True)
                    last.then_inc(att_made, 1)
                if stage_no == 6:
                    pe.wait_ge(masked_done, i + 1)
                    pe.wait_ge(state_done, i + 1)
                    if j == 0:
                        pe.wait_ge(kv_kept, i + 2)
                    for h in (0, 2, 1, 3):
                        p, hh = h // 2, h % 2
                        rows = slice(GP * hh, GP * hh + GK)
                        cols = slice(GV * p, GV * p + GV)
                        o_bank = bank[3 * (1 + hh)]
                        nc.tensor.matmul(o_bank[:, cols], att[:, h, :], gin[:, j, WB + GV * h:WB + GV * h + GV],
                                         start=True, stop=False, skip_group_check=True)
                        for c in range(2):
                            last = nc.tensor.matmul(o_bank[CH * c:CH * c + CH, cols], qkT[rows, j, p, CH * c:CH * c + CH],
                                                    state[rows, 2 * j + c, p, :], start=False, stop=(c == 1), skip_group_check=True)
                    last.then_inc(o_made, 1)
                if stage_no == 7:
                    pe.wait_ge(y_done, i + 3)
                    if j == 1:
                        pe.wait_ge(y_kept, i + 1)
                    for c in range(3):
                        last = nc.tensor.transpose(bank[0][:, c * P:(c + 1) * P], flat(osb[:, :, :])[:, c * P:(c + 1) * P], ident)
                    last.then_inc(y_turned, 1)

            with pe.Fori(0, 2) as it:
                for b in range(2):
                    for t in range(T):
                        pe.wait_ge(proj_kept, it * 16 + (NC_UNITS + 8 * b + t - 1))
                        if t == 0:
                            pe.wait_ge(w_ready, it * 16 + (K * (5 + b)))
                        project(bank[4 + t % 2][:, 0:WB], t, b, WB).then_inc(proj_made, 1)
                        if t < 7:
                            gla(t + 1, it * 4 + 2 * b, 0, it * 2 + b)
                        if t > 0:
                            gla(t, it * 4 + (2 * b + 1), 1, it * 2 + b)

            pe.wait_ge(rdiag_ready, 1)
            pe.wait_ge(y_kept, T + 1)
            for c in range(2):
                last = nc.tensor.matmul(pA[:, c, :], ones, flat(rdiag[:, 4 * c:4 * c + 4, :]), start=True, stop=True)
            last.then_inc(rstdB_made, 1)
            for u in range(8):
                m, half = u // 2, u % 2
                pe.wait_ge(w_ready, 9 * K if m < 3 else 10 * K)
                if u < 2:
                    pe.wait_ge(proj_kept, NU)
                else:
                    pe.wait_ge(pf_kept, u - 1)
                buf, col = (0, m * P) if m < 3 else (1, 0)
                for k in range(K):
                    for n, (w, a) in enumerate(((w_hi, hT_hi), (w_hi, hT_lo), (w_lo, hT_hi))):
                        last = nc.tensor.matmul(bank[4 + u % 2], w[:, buf, k, col:col + P], a[:, k, 512 * half:512 * half + 512],
                                                start=(k == 0 and n == 0), stop=(k == K - 1 and n == 2))
                last.then_inc(pf_made, 1)
            pe.wait_ge(wpd_in, 4 * 16)
            for u in range(4):
                m, half = u // 2, u % 2
                pe.wait_ge(pooled_done, m + 1)
                if u >= 2:
                    pe.wait_ge(yb_done, u - 1)
                nc.tensor.matmul(bank[6 + half], wpd[:, m, :], uT[:, m, PADL + 512 * half:PADL + 512 * half + 512],
                                 start=True, stop=True).then_inc(yb_made, 1)

            def pair(p):
                made = [0, 0]

                def turn(sources, par, reader_done=None):
                    pe.wait_ge(tb_kept[par], p * NG + (made[par] + 1))
                    for n, src in enumerate(sources):
                        last = nc.tensor.transpose(bank[4 + par][:, n * P:(n + 1) * P], src, ident)
                    made[par] += 1
                    return last

                pe.wait_ge(qk_split, p + 1)
                for hh in range(2):
                    for w in range(2):
                        for g in range(2):
                            last = turn([qk_st[:, w, hh, 4 * g + n, :] for n in range(4)], g)
                            last.then_inc(tb_made[g], 1)
                turned = [0]

                def logits(s):
                    hh, t = s // T, s % T
                    pe.wait_ge(logits_read, p * 16 + (s + 1))
                    if t == 0:
                        for par in range(2):
                            pe.wait_ge(tb_kept[par], p * NG + (2 * hh + 3))
                    width = (t + 1) * P
                    dst = (pA, pB)[s % 2]
                    for c in range(0, width, 512):
                        w = min(512, width - c)
                        for m in range(2):
                            last = nc.tensor.matmul(dst[:, c // 512, 0:w], qT[:, hh, tiles(t)], kT[:, hh, m, c:c + w],
                                                    start=(m == 0), stop=(m == 1))
                    last.then_inc(logits_made, 1)

                kept_at = {}

                def turn_probs(s):
                    t = s % T
                    pe.wait_ge(prob_done, p * 16 + (s + 1))
                    kept_at[s] = []
                    gs = groups(t)
                    for n, grp in enumerate(gs):
                        par = turned[0] % 2
                        turned[0] += 1
                        last = turn([prob[:, s % 2, kt * P:(kt + 1) * P] for kt in grp], par)
                        last.then_inc(tb_made[par], 1)
                        kept_at[s].append((par, made[par] + 1))

                def pv(s):
                    hh, t = s // T, s % T
                    pe.wait_ge(pv_kept, p * 16 + (s + 1))
                    if s == 0:
                        pe.wait_ge(v_in, p * 16 + 16)
                    for par, n in kept_at[s]:
                        pe.wait_ge(tb_kept[par], p * NG + n)
                    for kt in range(t + 1):
                        last = nc.tensor.matmul(bank[6 + s % 2][HD * hh:HD * hh + HD, 0:P], v[:, kt, HD * hh:HD * hh + HD],
                                                probT[:, s % 2, kt, :], start=(kt == 0), stop=(kt == t))
                    last.then_inc(pv_made, 1)

                for s in range(2 * T + 2):
                    if s < 2 * T:
                        logits(s)
                    if 1 <= s <= 2 * T:
                        turn_probs(s - 1)
                    if s >= 2:
                        pv(s - 2)
                pe.wait_ge(gate_done, p + 1)
                for g in range(2):
                    last = turn([gate[:, 4 * g + n, :] for n in range(4)], g)
                    last.then_inc(tb_made[g], 1)
                assert made == [NG, NG], (made, NG)

            with pe.Fori(0, PAIRS - 1) as p:
                pair(p)
            pair(PAIRS - 1)

            for k in range(K):
                pe.wait_ge(wo_ready, k + 1)
                pe.wait_ge(mixhi_ready, k + 1)
                pe.wait_ge(mixlo_ready, k + 1)
                if k == 0:
                    for par in range(2):
                        pe.wait_ge(tb_kept[par], PAIRS * NG + 1)
                for t in range(T):
                    for n, (a, w) in enumerate(((mix_hi, wo_hi), (mix_hi, wo_lo), (mix_lo, wo_hi))):
                        last = nc.tensor.matmul(bank[t], a[:, OUT_ORDER[k], tiles(t)], w[:, k, :],
                                                start=(k == 0 and n == 0), stop=(k == K - 1 and n == 2))
                    if k == K - 1:
                        last.then_inc(out_made, 1)
            for t in range(T):
                if t == 0:
                    pe.wait_ge(wo_ready, 2 * K)
                pe.wait_ge(out_added, t + 1)
                for k in range(K):
                    for n, (a, w) in enumerate(((mix_hi, wo_hi2), (mix_hi, wo_lo2), (mix_lo, wo_hi2))):
                        last = nc.tensor.matmul(bank[t], a[:, OUT_ORDER[k], tiles(t)], w[:, k, :],
                                                start=(k == 0 and n == 0), stop=(k == K - 1 and n == 2))
                last.then_inc(out_made, 1)

        @block.scalar
        def _(act):
            own = Chain(act, act_done)

            for t in range(T):
                act.wait_ge(x_in[t % 2], 16 * (t // 2 + 1))
                nc.scalar.activation(x_ring[:, t % 2, :], x_ring[:, t % 2, :], ACT.Square,
                                     accum_out=ssx[:, t:t + 1]).then_inc(x_squared, 1)
            for s, n in ((y_kept, 1), (y_out, 16), (tb_kept[0], 1), (pv_kept, 2)):
                act.sem_inc(s, n)
            for t in range(T):
                act.wait_ge(idx_turned, t + 1)
                if t >= T0:
                    nc.scalar.activation(iqT[:, :, (t - T0) * P:(t - T0 + 1) * P],
                                         bank[t].rearrange("p (h n) -> p h n", h=IH), ACT.Copy).then_inc(idx_kept, 1)
                nc.scalar.activation(ikT[:, :, tiles(t)],
                                     bank[t if t < T0 else t - T0][:, 0:2 * P].rearrange("p (m n) -> p m n", m=2),
                                     ACT.Copy).then_inc(idx_kept, 1)

            def relu(n):
                t = T0 + n // IH
                act.wait_ge(dots_made, n + 1)
                if n >= 2:
                    act.wait_ge(dots_added, n - 1)
                src = flat((pA, pB)[n % 2][:, :, :])
                nc.scalar.activation(relus[:, n % 2, 0:(t + 1) * P], src[:, 0:(t + 1) * P], ACT.Relu).then_inc(dots_relu, 1)

            def keep(u_off, u, t, func, spills):
                act.wait_ge(proj_made, u_off + (u + 1))
                if spills is not None:
                    act.wait_ge(spilled[u % 4], spills)
                nc.scalar.activation(evac[:, u % 4, :], bank[4 + u % 2][:, 0:WB], func,
                                     scale=rstd[:, t:t + 1]).then_inc(proj_kept, 1)

            for n in range(1, 4):
                for t in range(T):
                    u = (n - 1) * T + t
                    if n == 1 and t < TS:
                        for h in range(IH):
                            relu(t * IH + h)
                    keep(0, u, t, ACT.Silu if n == 3 else ACT.Copy, 16 * (u // 4) if u >= 4 else None)
            act.wait_ge(gla_clear, 1)

            def turn_in(i, tile_at):
                nc.scalar.activation(ggs[:, :], gg[:, bass.ds(tile_at, 1), :].rearrange("p a n -> p (a n)"), ACT.Copy).then_inc(ggs_ready, 1)

            def gla(stage_no, i, j):
                if stage_no == 1:
                    act.wait_ge(ggT_made, i + 1)
                    nc.scalar.activation(ggT[0:RANK, :], bank[0][0:RANK, 0:P], ACT.Copy).then_inc(ggT_kept, 1)
                if stage_no == 2:
                    act.wait_ge(z_made, i + 1)
                    z = bank[1][:, 0:GH * GK].rearrange("p (h n) -> p h n", h=GH)
                    nc.scalar.activation(sp_r[:, :, :], z, ACT.Relu, scale=-1.0)
                    own.link(nc.scalar.activation(sp_a[:, :, :], z, ACT.Abs))
                    own.link(nc.scalar.activation(sp_a[:, :, :], sp_a[:, :, :], ACT.Exp, scale=-1.0))
                    nc.scalar.activation(sp_a[:, :, :], sp_a[:, :, :], ACT.Ln, bias=1.0).then_inc(sp_kept, 1)
                if stage_no == 3:
                    act.wait_ge(sums_made, i + 1)
                    upto = bank[2][:, 0:256].rearrange("p (h n) -> p h n", h=GH)[:, :, 0:GK]
                    after = bank[2][:, 256:512].rearrange("p (h n) -> p h n", h=GH)[:, :, 0:GK]
                    nc.scalar.activation(eb[:, :, :], upto, ACT.Exp, scale=-1.0 / TAU)
                    nc.scalar.activation(enb[:, :, :], upto, ACT.Exp, scale=1.0 / TAU)
                    nc.scalar.activation(ed[:, :, :], after, ACT.Exp, scale=-1.0 / TAU)
                    nc.scalar.activation(gdec[:, :], bank[0][:, 0:4], ACT.Exp, scale=-1.0 / TAU).then_inc(exps_kept, 1)
                if stage_no == 4:
                    act.wait_ge(qkT_made, i + 1)
                    src = bank[3].rearrange("p (a n) -> p a n", a=4)
                    nc.scalar.activation(qkT[:, j, 0:2, :], src[:, 0:2, :], ACT.Copy, scale=float(GK) ** -0.5)
                    nc.scalar.activation(qkT[:, j, 2:4, :], src[:, 2:4, :], ACT.Copy).then_inc(qkT_kept, 1)
                    for c in range(2):
                        last = nc.scalar.activation(flat(kv[:, j, c, :, :]), bank[6 + c][:, 0:2 * GV], ACT.Copy)
                    last.then_inc(kv_kept, 1)
                if stage_no == 5:
                    act.wait_ge(att_made, i + 1)
                    for hh in range(2):
                        dst = att[:, :, :].rearrange("p (a b) n -> p b a n", b=2)[:, hh]
                        src = bank[2 - hh][:, 0:2 * P].rearrange("p (a n) -> p a n", a=2)
                        for c in range(2):
                            r = slice(CH * c, CH * c + CH)
                            last = nc.scalar.activation(dst[r, :, r], src[r, :, r], ACT.Copy)
                    last.then_inc(att_kept, 1)
                if stage_no == 6:
                    act.wait_ge(o_made, i + 1)
                    for h in range(GH):
                        nc.scalar.activation(osq[:, h, :], bank[3 * (1 + h % 2)][:, GV * (h // 2):GV * (h // 2) + GV], ACT.Square,
                                             accum_out=gss[:, h:h + 1])
                    for hh in range(2):
                        last = nc.scalar.activation(osb[:, :, :].rearrange("p (a b) n -> p b a n", b=2)[:, hh],
                                                    bank[3 * (1 + hh)][:, 0:2 * GV].rearrange("p (a n) -> p a n", a=2), ACT.Copy)
                    last.then_inc(o_kept, 1)
                if stage_no == 7:
                    act.wait_ge(y_turned, i + 1)
                    act.wait_ge(y_out, i * 16 + 16)
                    nc.scalar.activation(flat(yT[:, :, :]), bank[0][:, 0:3 * P], ACT.Copy).then_inc(y_kept, 1)

            with act.Fori(0, 2) as it:
                own.loop(it, 2 * 2 * 2)
                for b in range(2):
                    for t in range(T):
                        if t < 2:
                            if t == 1:
                                act.wait_ge(ggT_made, it * 4 + (2 * b + 1))
                            turn_in(None, it * 4 + (2 * b + t))
                        act_u = NC_UNITS + 8 * b + t
                        keep(it * 16, act_u, t, ACT.Copy, it * 64 + 16 * (act_u // 4))
                        if t < 7:
                            gla(t + 1, it * 4 + 2 * b, 0)
                        if t > 0:
                            gla(t, it * 4 + (2 * b + 1), 1)
                own.end(2)

            for i in range(4):
                act.wait_ge(spilled[i], NBK)
            act.wait_ge(rstdB_made, 1)
            nc.scalar.activation(rstdB[:, :], flat(pA[:, :, :]), ACT.Copy).then_inc(rstdB_ready, 1)

            def squares(p):
                act.wait_ge(qk_in, p * 32 + 32)
                for w in range(2):
                    last = nc.scalar.activation(flat(sq[:, w, :, :]), flat(raw_qk[:, w, :, :]), ACT.Square)
                last.then_inc(qk_squared, 1)

            squares(0)
            for u in range(4, 8):
                act.wait_ge(pf_kept, u + 1)
                z = zT[:, (u - 4) // 2, 512 * (u % 2):512 * (u % 2) + 512]
                nc.scalar.activation(z, z, ACT.Silu).then_inc(silu_done, 1)

            def pair(p, more):
                kept = 0

                def stack(hh, w):
                    act.wait_ge(tb_made[0], p * NG + (kept + 1))
                    if w == 0:
                        return nc.scalar.activation(qT[:, hh, 0:512], bank[4], ACT.Copy)
                    nc.scalar.activation(kT[:, hh, 0, 0:512], bank[4], ACT.Copy)
                    nc.scalar.activation(kT[0:HD, hh, 1, 0:512], bank[4][HD:P, :], ACT.Copy)
                    return nc.scalar.activation(kT[HD:P, hh, 1, 0:512], bank[4][0:HD, :], ACT.Copy)

                for hh in range(2):
                    for w in range(2):
                        stack(hh, w).then_inc(tb_kept[0], 1)
                        kept += 1
                c = 0
                for s in range(2 * T + 2):
                    if s < 2 * T:
                        t = s % T
                        act.wait_ge(max_ready, p * 16 + (s + 1))
                        nc.scalar.activation(prob[:, s % 2, 0:(t + 1) * P], prob[:, s % 2, 0:(t + 1) * P], ACT.Exp,
                                             bias=nmx[:, s % 2:s % 2 + 1], accum_out=rsum[:, t, s // T:s // T + 1]).then_inc(prob_done, 1)
                    if 1 <= s <= 2 * T:
                        for grp in groups((s - 1) % T):
                            if c % 2 == 0:
                                act.wait_ge(tb_made[0], p * NG + (kept + 1))
                                act.wait_ge(pv_made, p * 16 + s)
                                nc.scalar.activation(flat(probT[:, (s - 1) % 2, grp[0]:grp[0] + len(grp), :]),
                                                     bank[4][:, 0:len(grp) * P], ACT.Copy).then_inc(tb_kept[0], 1)
                                kept += 1
                            c += 1
                    if s == 2 * T:
                        act.wait_ge(z_in, p * 16 + 16)
                        nc.scalar.activation(flat(gate[:, :, :]), flat(gate[:, :, :]), ACT.Silu).then_inc(gate_silu, 1)
                    if s >= 2:
                        n = s - 2
                        hh, t = n // T, n % T
                        act.wait_ge(pv_made, p * 16 + (n + 3))
                        if n == 0:
                            act.wait_ge(mixA_done, p + 1)
                        r = slice(HD * hh, HD * hh + HD)
                        nc.scalar.activation(oT[r, tiles(t)], bank[6 + n % 2][r, 0:P], ACT.Copy).then_inc(pv_kept, 1)
                    if s == 4 and more:
                        act.wait_ge(qk_split, p + 1)
                        squares(p + 1)

            with act.Fori(0, PAIRS - 1) as p:
                pair(p, True)
            pair(PAIRS - 1, False)

            for k, c in enumerate(OUT_ORDER):
                if c >= PAIRS:
                    act.wait_ge(mix_in[k % 2], 16 * (k // 2 + 1))
                act.wait_ge(mixA_done, PAIRS + 1)
                src = mix_raw[:, k % 2, :] if c >= PAIRS else mixA[:, c, :]
                nc.scalar.activation(mix_hi[:, c, :], src, ACT.Copy).then_inc(mixhi_ready, 1)

        @block.vector
        def _(dve):
            own = Chain(dve, dve_done)
            link = own.link
            vec = nc.vector
            dve.wait_ge(const_in, 16)
            for k in range(K):
                dve.wait_ge(xT_in[k % 4], 16 * (k // 4 + 1))
                link(vec.tensor_scalar(hT_hi[:, k, :], xT_raw[:, k % 4, :], norm_g[:, k:k + 1], None, ALU.mult))
                vec.scalar_tensor_tensor(out=hT_lo[:, k, :], in0=xT_raw[:, k % 4, :], scalar=norm_g[:, k:k + 1],
                                         in1=hT_hi[:, k, :].bitcast(F32), op0=ALU.mult, op1=ALU.subtract).then_inc(hT_ready, 1)
            for s, n in ((y_done, 2), (tb_kept[1], 1), (logits_read, 2), (pv_made, 2), (mixA_done, 1)):
                dve.sem_inc(s, n)
            dve.wait_ge(rstd_ready, 1)
            for t in range(T):
                dve.wait_ge(idx_made, t + 1)
                if t >= 2:
                    dve.wait_ge(idx_turned, t - 1)
                r = rstd[:, t:t + 1]
                src = bank[t][:, 0:5 * IDIM].rearrange("p (h n) -> p h n", h=5)
                st = stage[:, t % 2, :, :]
                link(vec.tensor_scalar(st[:, 0:5, 0:IDIM].bitcast(F32R), src, r, None, ALU.mult))
                link(vec.scalar_tensor_tensor(out=st[:, 0:5, IDIM:P], in0=src, scalar=r, in1=st[:, 0:5, 0:IDIM],
                                              op0=ALU.mult, op1=ALU.subtract))
                vec.tensor_copy(st[:, 5, 0:IDIM], st[:, 4, IDIM:P])
                vec.tensor_copy(st[:, 5, IDIM:P], st[:, 4, 0:IDIM])
                vec.tensor_scalar(gg[:, t, :], bank[t][:, IDXW - RANK:IDXW], r, None, ALU.mult)
                vec.tensor_scalar(iw[:, t, :], bank[t][:, 5 * IDIM:5 * IDIM + IH], r, IH ** -0.5, ALU.mult, ALU.mult).then_inc(idx_staged, 1)
            for n in range(NDOT):
                t, h = T0 + n // IH, n % IH
                sc = scores[:, SOFF[t]:SOFF[t + 1]]
                wgt = iw[:, t, h:h + 1]
                dve.wait_ge(dots_relu, n + 1)
                if h == 0:
                    vec.tensor_scalar(sc, relus[:, n % 2, 0:(t + 1) * P], wgt, None, ALU.mult).then_inc(dots_added, 1)
                else:
                    dve.wait_ge(dots_added, n)
                    vec.scalar_tensor_tensor(out=sc, in0=relus[:, n % 2, 0:(t + 1) * P], scalar=wgt, in1=sc,
                                             op0=ALU.mult, op1=ALU.add).then_inc(dots_added, 1)
                if h == IH - 1:
                    dve.wait_ge(dots_added, n + 1)
                    diag = scores[:, SOFF[t] + t * P:SOFF[t + 1]]
                    own.step(vec.tensor_tensor(diag, diag, causal, ALU.add))
            own.wait()

            def count(thresholds, op, dst):
                for t in range(T0, T):
                    at = thresholds if isinstance(thresholds, float) else thresholds[:, t - T0:t - T0 + 1]
                    last = vec.tensor_scalar(out=seen[:, SOFF[t]:SOFF[t + 1]], in0=scores[:, SOFF[t]:SOFF[t + 1]], scalar1=at,
                                             scalar2=None, op0=op, op1=ALU.add, accum_out=dst[:, t - T0:t - T0 + 1])
                link(last)

            link(vec.memset(bit[:, :], 1 << 30))
            count(0.0, ALU.is_ge, cnt)
            link(vec.tensor_scalar(pat[:, :], cnt[:, :], float(TOPK), None, ALU.is_lt))
            link(vec.tensor_scalar(pat[:, :].bitcast(I32), pat[:, :].bitcast(I32), 31, 31, ALU.arith_shift_left, ALU.arith_shift_right))
            with dve.Fori(0, 31) as i:
                own.loop(i, 5)
                link(vec.tensor_tensor(cand[:, :], pat[:, :], bit[:, :], ALU.bitwise_xor))
                count(cand[:, :].bitcast(F32), ALU.is_ge, cnt)
                link(vec.scalar_tensor_tensor(out=inc[:, :], in0=cnt[:, :], scalar=float(TOPK), in1=bit[:, :], op0=ALU.is_ge, op1=ALU.mult))
                link(vec.tensor_tensor(pat[:, :], pat[:, :], inc[:, :], ALU.bitwise_xor))
                link(vec.tensor_scalar(bit[:, :], bit[:, :], 1, None, ALU.logical_shift_right))
                own.end(31)
            thr = pat[:, :].bitcast(F32)
            count(thr, ALU.is_gt, cnt)
            link(vec.tensor_scalar(need[:, :], cnt[:, :], -1.0, float(TOPK), ALU.mult, ALU.add))
            for t in range(T0, T):
                sc, m = scores[:, SOFF[t]:SOFF[t + 1]], mask[:, MOFF[t]:MOFF[t + 1]]
                width, at = (t + 1) * P, slice(t - T0, t - T0 + 1)
                eq, upto = relus[:, 0, 0:width], relus[:, 1, 0:width]
                link(vec.tensor_scalar(eq, sc, thr[:, at], None, ALU.is_equal))
                link(vec.tensor_tensor_scan(out=upto, data0=eq, data1=eq, initial=0.0, op0=ALU.add, op1=ALU.max))
                link(vec.scalar_tensor_tensor(out=eq, in0=upto, scalar=need[:, at], in1=eq, op0=ALU.is_le, op1=ALU.mult))
                link(vec.scalar_tensor_tensor(out=upto, in0=sc, scalar=thr[:, at], in1=eq, op0=ALU.is_gt, op1=ALU.add))
                link(vec.tensor_scalar(m, upto, -NEGM, NEGM, ALU.mult, ALU.add))
            link(vec.memset(mask[:, MOFF[1]:MOFF[1] + P], 0.0))
            for t in range(T0):
                vec.tensor_copy(mask[:, MOFF[t] + t * P:MOFF[t + 1]], causal)
            for t in range(T):
                last = vec.tensor_scalar(rdiag[:, t, :], ident, rstd[:, t:t + 1], None, ALU.mult)
            link(last)
            dve.sem_inc(rdiag_ready, 1)

            vec.memset(uT[:, :, 0:PADL], 0.0)
            dve.wait_ge(rstdB_made, 1)
            link(vec.memset(win[:, :, 0:PADL], 0.0))
            dve.wait_ge(rstdB_ready, 1)

            def keep(u):
                dve.wait_ge(pf_made, u + 1)
                m, half = u // 2, u % 2
                cols = slice(512 * half, 512 * half + 512)
                dst = uT[:, m, PADL + 512 * half:PADL + 512 * half + 512] if m < 2 else zT[:, m - 2, cols]
                vec.tensor_tensor(dst, bank[4 + u % 2], rstdB[:, cols], ALU.mult).then_inc(pf_kept, 1)

            def add_shifted(dst, src, shift, rows):
                link(vec.tensor_tensor(dst[rows, shift:PADL + S], src[rows, shift:PADL + S], src[rows, 0:PADL + S - shift], ALU.add))

            def pool(m):
                dve.wait_ge(pf_kept, 2 * m + 2)
                a, b, u_ = win[:, 0, :], win[:, 1, :], uT[:, m, :]
                both, low, high = slice(0, P), slice(0, HD), slice(HD, P)
                add_shifted(a, u_, 1, both)
                if m == 0:
                    add_shifted(b, a, 2, high)
                else:
                    add_shifted(b, a, 2, both)
                    add_shifted(a, b, 4, both)
                    add_shifted(b, a, 8, high)
                for r, w in ((low, a), (high, b)):
                    head, rest = slice(PADL, 2 * PADL), slice(2 * PADL, PADL + S)
                    link(vec.tensor_tensor(w[r, head], w[r, head], pool_cnt[r, m, :], ALU.mult))
                    own.step(vec.tensor_tensor(u_[r, head], w[r, head], u_[r, head], ALU.subtract))
                    link(vec.scalar_tensor_tensor(out=u_[r, rest], in0=w[r, rest], scalar=pool_w1[r, m:m + 1], in1=u_[r, rest],
                                                  op0=ALU.mult, op1=ALU.subtract))
                dve.sem_inc(pooled_done, 1)

            for u in range(4):
                keep(u)
            pool(0)
            for u in range(4, 6):
                keep(u)
            pool(1)
            for u in range(6, 8):
                keep(u)

            def sums(p):
                dve.wait_ge(qk_squared, p + 1)
                link(vec.tensor_reduce(ssq[:, :], sq[:, :, :, :].rearrange("p w t (h n) -> p (w t h) n", h=2), axis=AX.X, op=ALU.add))
                dve.sem_inc(qk_summed, 1)

            sums(0)
            for u in range(4):
                m, half = u // 2, u % 2
                dve.wait_ge(yb_made, u + 1)
                dve.wait_ge(silu_done, u + 1)
                z = zT[:, m, 512 * half:512 * half + 512]
                vec.scalar_tensor_tensor(out=z, in0=bank[6 + half], scalar=pscale[:, m:m + 1], in1=z, op0=ALU.mult, op1=ALU.mult).then_inc(yb_done, 1)

            def pair(p, more, links):
                kept = 0
                for hh in range(2):
                    for w in range(2):
                        dve.wait_ge(tb_made[1], p * NG + (kept + 1))
                        if w == 0:
                            last = vec.tensor_copy(qT[:, hh, 512:1024], bank[5])
                        else:
                            vec.tensor_copy(kT[:, hh, 0, 512:1024], bank[5])
                            vec.tensor_copy(kT[0:HD, hh, 1, 512:1024], bank[5][HD:P, :])
                            last = vec.tensor_copy(kT[HD:P, hh, 1, 512:1024], bank[5][0:HD, :])
                        last.then_inc(tb_kept[1], 1)
                        kept += 1
                c = 0
                for s in range(2 * T + 1):
                    if s < 2 * T:
                        t = s % T
                        width = (t + 1) * P
                        dve.wait_ge(logits_made, p * 16 + (s + 1))
                        for par, n in turned_at(s - 2) if s >= 2 else ():
                            dve.wait_ge(tb_made[par], p * NG + n)
                        alone(dve)
                        vec.tensor_tensor_reduce(out=prob[:, s % 2, 0:width], in0=flat((pA, pB)[s % 2][:, :, :])[:, 0:width],
                                                 in1=mask[:, MOFF[t]:MOFF[t + 1]], scale=1.0, scalar=NEG, op0=ALU.add, op1=ALU.max,
                                                 accum_out=mx[:, s % 2:s % 2 + 1]).then_inc(logits_read, 1)
                        dve.wait_ge(logits_read, p * 16 + (s + 3))
                        vec.tensor_scalar(nmx[:, s % 2:s % 2 + 1], mx[:, s % 2:s % 2 + 1], -1.0, None, ALU.mult).then_inc(max_ready, 1)
                    if s >= 1:
                        for grp in groups((s - 1) % T):
                            if c % 2 == 1:
                                dve.wait_ge(tb_made[1], p * NG + (kept + 1))
                                dve.wait_ge(pv_made, p * 16 + s)
                                vec.tensor_copy(flat(probT[:, (s - 1) % 2, grp[0]:grp[0] + len(grp), :]),
                                                bank[5][:, 0:len(grp) * P]).then_inc(tb_kept[1], 1)
                                kept += 1
                            c += 1
                    if s == 8 and more:
                        sums(p + 1)
                dve.wait_ge(prob_done, p * 16 + 16)
                link(vec.reciprocal(flat(rinv[:, :, :]), flat(rsum[:, :, :])))
                dve.wait_ge(gate_silu, p + 1)
                g4 = gate[:, :, :].rearrange("p t (h n) -> p (t h) n", h=2)
                vec.tensor_tensor(g4, g4, flat(rinv[:, :, :])[:, :, None].broadcast_to([P, 2 * T, HD]), ALU.mult).then_inc(gate_done, 1)
                dve.wait_ge(pv_kept, p * 16 + 18)
                for g in range(2):
                    dve.wait_ge(tb_made[g], p * NG + NG)
                    vec.tensor_tensor(mixA[:, p, 512 * g:512 * g + 512] if isinstance(p, int) else
                                      mixA[:, bass.ds(p, 1), 512 * g:512 * g + 512].rearrange("p a n -> p (a n)"),
                                      bank[4 + g], oT[:, 512 * g:512 * g + 512], ALU.mult).then_inc(tb_kept[g], 1)
                for g in range(2):
                    dve.wait_ge(tb_kept[g], p * NG + (NG + 1))
                dve.sem_inc(mixA_done, 1)

            with dve.Fori(0, PAIRS - 1) as p:
                own.loop(p, 2)
                pair(p, True, 2)
                own.end(PAIRS - 1)
            pair(PAIRS - 1, False, 1)

            for k, c in enumerate(OUT_ORDER):
                dve.wait_ge(mixhi_ready, k + 1)
                src = mix_raw[:, k % 2, :] if c >= PAIRS else mixA[:, c, :]
                vec.tensor_tensor(mix_lo[:, c, :], src, mix_hi[:, c, :].bitcast(F32), ALU.subtract).then_inc(mixlo_ready, 1)
            for u in range(2 * T):
                dve.wait_ge(out_made, u + 1)
                dve.wait_ge(res_in[u % 4], 16 * (u // 4 + 1))
                if u >= 4:
                    dve.wait_ge(out_out[u % 4], 16 * (u // 4))
                vec.tensor_tensor(outb[:, u % 4, :], bank[u % T], res[:, u % 4, :], ALU.add).then_inc(out_added, 1)

        @block.gpsimd
        def _(pool):
            own = Chain(pool, pool_done, alone)
            link = own.link
            gp = nc.gpsimd

            def split_w(buf, k, width, arrived):
                pool.wait_ge(w_in[k], arrived)
                if not isinstance(arrived, int):
                    alone(pool)
                link(gp.tensor_scalar(w_hi[:, buf, k, 0:width], w_raw[:, k, 0:width], 1.0, 1.0, ALU.mult, ALU.mult))
                gp.tensor_tensor(w_lo[:, buf, k, 0:width], w_raw[:, k, 0:width], w_hi[:, buf, k, 0:width].bitcast(F32),
                                 ALU.subtract).then_inc(w_ready, 1)

            own.step(gp.memset(neghalf[:, :], -0.5))
            for n in range(5):
                if n == 2:
                    pool.wait_ge(x_squared, T)
                    link(gp.tensor_scalar(rtmp[:, 0:T], ssx[:, :], 1.0 / D, EPS, ALU.mult, ALU.add))
                    gp.tensor_tensor(rstd[:, :], rtmp[:, 0:T], neghalf[:, 0:T], ALU.pow).then_inc(rstd_ready, 1)
                    pool.wait_ge(idx_made, T)
                if n > 2:
                    pool.wait_ge(proj_made, T * (n - 2))
                for k in range(K):
                    split_w(n % 2, k, BLOCK_W[n], 16 * (n + 1))

            pool.wait_ge(dots_made, NDOT)
            for buf, val in ((nl, 0.0), (qs, 0.0), (ks, 0.0), (kd, 0.0), (att, 0.0)):
                gp.memset(buf[:, :, :], val)
            gp.memset(state[:, 4, :, :], 0.0)
            link(gp.memset(ggT[:, :], 1.0))
            pool.sem_inc(gla_clear, 1)

            def gla(stage_no, i, j, rounds):
                if stage_no == 2:
                    pool.wait_ge(sp_kept, i + 1)
                    gp.tensor_tensor(nl[:, :, 0:GK], sp_a[:, :, :], sp_r[:, :, :], ALU.add).then_inc(nl_done, 1)
                if stage_no == 3:
                    pool.wait_ge(exps_kept, i + 1)
                    pool.wait_ge(gin_in[j], rounds * 16 + 16)
                    q = gin[:, j, 0:GH * GK].rearrange("p (h n) -> p h n", h=GH)
                    k = gin[:, j, GH * GK:2 * GH * GK].rearrange("p (h n) -> p h n", h=GH)
                    gp.tensor_tensor(qs[:, :, 0:GK], q, eb[:, :, :], ALU.mult)
                    gp.tensor_tensor(ks[:, :, 0:GK], k, enb[:, :, :], ALU.mult)
                    gp.tensor_tensor(kd[:, :, 0:GK], k, ed[:, :, :], ALU.mult)
                    gp.tensor_scalar(dec[:, j, :], gdec[:, :], 1.0, 1.0, ALU.mult, ALU.mult).then_inc(scaled_done, 1)
                if stage_no == 4:
                    pool.wait_ge(kv_kept, i + 1)
                    pool.wait_ge(scaled_done, i + 1)
                    alone(pool)
                    if j == 0:
                        link(gp.tensor_scalar(flat(state[:, 0, :, :]), flat(state[:, 4, :, :]), 1.0, 1.0, ALU.mult, ALU.mult))
                    for c in range(2):
                        n = 2 * j + c
                        for p in range(2):
                            own.step(gp.tensor_scalar(state[:, n + 1, p, :], state[:, n, p, :], dec[:, j, 2 * p + c:2 * p + c + 1], 1.0, ALU.mult, ALU.mult))
                        own.wait()
                        own.step(gp.tensor_tensor(flat(state[:, n + 1, :, :]), flat(state[:, n + 1, :, :]), flat(kv[:, j, c, :, :]), ALU.add))
                        own.wait()
                    pool.sem_inc(state_done, 1)
                if stage_no == 5:
                    pool.wait_ge(att_kept, i + 1)
                    alone(pool)
                    gp.affine_select(out=att[:, :, :], in_=att[:, :, :], compare_op=ALU.is_ge, fill=0.0, base=0,
                                     pattern=[[0, GH], [1, P]], channel_multiplier=-1).then_inc(masked_done, 1)
                if stage_no == 6:
                    pool.wait_ge(o_kept, i + 1)
                    alone(pool)
                    link(gp.tensor_scalar(grs[:, :], gss[:, :], 1.0 / GV, EPS, ALU.mult, ALU.add))
                    link(gp.tensor_tensor(grs[:, :], grs[:, :], neghalf[:, 0:GH], ALU.pow))
                    link(gp.tensor_tensor(osb[:, :, :], osb[:, :, :], grs[:, :, None].broadcast_to([P, GH, GV]), ALU.mult))
                    link(gp.tensor_tensor(osb[:, :, :], osb[:, :, :], gain_o[:, None, :].broadcast_to([P, GH, GV]), ALU.mult))
                    z = gin[:, j, 2 * WB:3 * WB]
                    gp.tensor_tensor(flat(osb[:, :, :]), flat(osb[:, :, :]), z, ALU.mult).then_inc(y_done, 1)

            with pool.Fori(0, 2) as it:
                own.loop(it, 2 * (K + 1 + 2 * 6 + 2 * 4))
                for b in range(2):
                    pool.wait_ge(proj_made, it * 16 + T * (3 + b))
                    for t in range(T):
                        split_w((b + 1) % 2, t, WB, it * 32 + 16 * (6 + b))
                        if t < 7:
                            gla(t + 1, it * 4 + 2 * b, 0, it * 2 + b)
                        if t > 0:
                            gla(t, it * 4 + (2 * b + 1), 1, it * 2 + b)
                own.end(2)
            for i in range(4):
                pool.wait_ge(spilled[i], NBK)
            link(gp.memset(wpd[:, :, :], 0.0))
            pool.sem_inc(wpd_clear, 1)
            pool.wait_ge(proj_made, T * 7)
            for k in range(K):
                split_w(1, k, BLOCK_W[9], 16 * 10)

            def split_qk(p):
                pool.wait_ge(qk_in, p * 32 + 32)
                pool.wait_ge(qk_summed, p + 1)
                alone(pool)
                link(gp.tensor_scalar(rtmp[:, :], ssq[:, :], 1.0 / HD, EPS, ALU.mult, ALU.add))
                link(gp.tensor_tensor(rqk[:, :], rtmp[:, :], neghalf[:, :], ALU.pow))
                link(gp.tensor_scalar(rqk[:, 0:2 * T], rqk[:, 0:2 * T], HD ** -0.5, 1.0, ALU.mult, ALU.mult))
                for w in range(2):
                    raw = raw_qk[:, w, :, :].rearrange("p t (h n) -> p (t h) n", h=2)
                    nrm = sq[:, w, :, :].rearrange("p t (h n) -> p (t h) n", h=2)
                    link(gp.tensor_tensor(nrm, raw, rqk[:, 2 * T * w:2 * T * w + 2 * T, None].broadcast_to([P, 2 * T, HD]), ALU.mult))
                    link(gp.tensor_tensor(nrm, nrm, (qgain, kgain)[w][:, None, :].broadcast_to([P, 2 * T, HD]), ALU.mult))
                if not (isinstance(p, int) and p == 0):
                    for g in range(2):
                        pool.wait_ge(tb_made[g], p * NG + (4 - NG))
                    alone(pool)
                for w in range(2):
                    for hh in range(2):
                        st = qk_st[:, w, hh, :, :]
                        src = sq[:, w, :, HD * hh:HD * hh + HD]
                        link(gp.tensor_scalar(st[:, :, 0:HD].bitcast(F32R), src, 1.0, 1.0, ALU.mult, ALU.mult))
                        last = gp.tensor_tensor(st[:, :, HD:P], src, st[:, :, 0:HD], ALU.subtract)
                        own.step(last)
                own.wait()
                pool.sem_inc(qk_split, 1)

            SQ = 3 + 4 + 8
            split_qk(0)

            def split_wo(n, hi, lo):
                pool.wait_ge(wo_in[n % 4], 16 * (n // 4 + 1))
                k = n % K
                link(gp.tensor_scalar(hi[:, k, :], wo_raw[:, n % 4, :], 1.0, 1.0, ALU.mult, ALU.mult))
                gp.tensor_tensor(lo[:, k, :], wo_raw[:, n % 4, :], hi[:, k, :].bitcast(F32), ALU.subtract).then_inc(wo_ready, 1)

            for n in range(K):
                split_wo(n, wo_hi, wo_lo)
            with pool.Fori(0, PAIRS - 1) as p:
                own.loop(p, SQ)
                split_qk(p + 1)
                own.end(PAIRS - 1)
            for g in range(2):
                pool.wait_ge(tb_made[g], (PAIRS - 1) * NG + 4)
            for n in range(K, 2 * K):
                split_wo(n, wo_hi2, wo_lo2)


def kernel(x, norm_g, w_in, att_q_gain, att_k_gain, pool_w, pool_scale, gla_w_gate, gla_b_gate,
           gla_out_gain, w_out):
    import concourse.bacc as bacc
    from concourse.bass_utils import run_bass_kernel_spmd as run

    def cols(a, b):
        return np.asarray(w_in)[0][:, a:b]

    def rows(a, n):
        return np.ascontiguousarray(np.broadcast_to(np.asarray(a).reshape(1, n), (P, n)))

    at = np.cumsum([0, 384, 384, 384, 384, 256, 64, 4, 256, 256, 192, 192, 384, 16, 384])
    aq, _, _, _, iq, _, iw, pu, _, gq, _, gv, gg, gz, end = at
    w = np.concatenate([cols(iq, pu), cols(gg, gz), cols(gq, gg), cols(gz, end), cols(aq, iq), cols(pu, gq),
                        np.zeros((D, WCOLS - B0 - BW), np.float32)], axis=1)
    j, i = np.arange(P)[:, None], np.arange(P)[None, :]
    same = (j // CH) == (i // CH)
    tok = np.arange(PADL)
    wins = [(2, 4), (8, 16)]
    cnt_ = np.zeros((P, 2, PADL), np.float32)
    w1 = np.zeros((P, 2), np.float32)
    for m in range(2):
        for g in range(2):
            cnt_[HD * g:HD * g + HD, m] = (1.0 / np.minimum(tok + 1, wins[m][g])).astype(np.float32)
            w1[HD * g:HD * g + HD, m] = 1.0 / wins[m][g]
    const = np.concatenate([
        np.eye(P), np.where(i <= j, 0.0, NEG), (j <= i) & same, (j > i) & same, np.ones((P, P)),
        j // CH == np.arange(2)[None, :], cnt_.reshape(P, 2 * PADL), w1], axis=1).astype(np.float32)
    assert const.shape == (P, CONSTS)
    x0 = np.ascontiguousarray(np.asarray(x)[0])
    arrays = {
        "x": x0, "xT": np.ascontiguousarray(x0.T),
        "norm_g": np.ascontiguousarray(np.asarray(norm_g)[0].reshape(K, P).T),
        "w": np.ascontiguousarray(w), "const": const,
        "qgain": rows(att_q_gain, HD), "kgain": rows(att_k_gain, HD), "gain_o": rows(gla_out_gain, GV),
        "pscale": np.ascontiguousarray(np.asarray(pool_scale)[0].reshape(2, P).T),
        "w_gate": np.ascontiguousarray(np.asarray(gla_w_gate)[0]),
        "b_gate": np.ascontiguousarray(np.asarray(gla_b_gate)[0].reshape(1, GH * GK)),
        "pool_w": np.ascontiguousarray(np.asarray(pool_w)[0]),
        "w_out": np.ascontiguousarray(np.asarray(w_out)[0]),
    }
    nc = bacc.Bacc("TRN2", target_bir_lowering=False, num_devices=1)
    d = {n: nc.dram_tensor(f"in_{n}", a.shape, F32, kind="ExternalInput").ap() for n, a in arrays.items()}
    d["out"] = nc.dram_tensor("out_dram", (S, D), F32, kind="ExternalOutput").ap()
    program(nc, d)
    r = run(nc, [{f"in_{n}": a for n, a in arrays.items()}], core_ids=[0])
    return r.results[0]["out_dram"].reshape(1, S, D)
```

```python
from contextlib import ExitStack

import numpy as np
import concourse.bass as bass
from concourse import mybir

F32 = mybir.dt.float32
F32R = mybir.dt.float32r
BF16 = mybir.dt.bfloat16
U32 = mybir.dt.uint32
I32 = mybir.dt.int32
U8 = mybir.dt.uint8
ALU = mybir.AluOpType
ACT = mybir.ActivationFunctionType
AX = mybir.AxisListType

P = 128
S = 1024
D = 1024
T = S // P
K = D // P
EPS = 1e-6
HEADS, HD = 6, 64
PAIRS = HEADS // 2
IH, IDIM = 4, 64
TOPK = 256
T0 = TOPK // P
TS = T - T0
GH, GK, GV, RANK = 4, 48, 96, 16
GP = 64
TAU = 16.0
CH = 64
WB = 384
NEG = -3.0e38
NEGM = -1.0e30

IDXW = IH * IDIM + IDIM + IH + RANK
C0 = IDXW
CW = 3 * WB
A0 = C0 + CW
AW = 4 * WB
B0 = A0 + AW
BW = 512
WCOLS = B0 + 2 * WB
BLOCK_AT = [0] + [C0 + WB * i for i in range(3)] + [A0 + WB * i for i in range(6)]
BLOCK_W = [IDXW] + [WB] * 8 + [BW - WB]
NBLK = len(BLOCK_W)
NC_UNITS = 3 * T
MOFF = [P * t * (t + 1) // 2 for t in range(T + 1)]
SOFF = [MOFF[t] - MOFF[T0] for t in range(T + 1)]
PADL = 16

CI, CC, CTI, CTS, CON, CCH, CNT, CW1 = 0, 128, 256, 384, 512, 640, 642, 674
CONSTS = 676


class Chain:

    def __init__(self, engine, sem, after_loop_wait=None):
        self.engine, self.sem, self.n, self.off = engine, sem, 0, 0
        self.after_loop_wait = after_loop_wait

    def step(self, ins):
        ins.then_inc(self.sem, 1)
        self.n += 1

    def wait(self):
        self.engine.wait_ge(self.sem, self.off + self.n)
        if self.after_loop_wait and not isinstance(self.off, int):
            self.after_loop_wait(self.engine)

    def link(self, ins):
        self.step(ins)
        self.wait()

    def loop(self, i, stride):
        self.off, self.began, self.stride = i * stride, self.n, stride

    def end(self, rounds):
        assert self.n - self.began == self.stride, (self.n - self.began, self.stride)
        self.off = 0
        self.n += self.stride * (rounds - 1)


def program(nc, d):
    ctx = ExitStack()
    with ctx:
        def sb(name, shape, dt=F32):
            return ctx.enter_context(nc.sbuf_tensor(name, shape, dt))

        def sem(name):
            return ctx.enter_context(nc.semaphore(name))

        const = sb("const", [P, CONSTS])
        ident = const[:, CI:CI + P]
        causal = const[:, CC:CC + P]
        tri_upto = const[:, CTI:CTI + P]
        tri_after = const[:, CTS:CTS + P]
        ones = const[:, CON:CON + P]
        in_chunk = const[:, CCH:CCH + 2]
        pool_cnt = const[:, CNT:CNT + 32].rearrange("p (m t) -> p m t", m=2)
        pool_w1 = const[:, CW1:CW1 + 2]
        norm_g = sb("norm_g", [P, K])
        mask = sb("mask", [P, MOFF[T]], BF16)
        iw = sb("iw", [P, T, IH])
        gg = sb("gg", [P, T, RANK])
        rstd = sb("rstd", [P, T])
        rtmp = sb("rtmp", [P, 32])
        neghalf = sb("neghalf", [P, 32])
        qgain = sb("qgain", [P, HD])
        kgain = sb("kgain", [P, HD])
        gain_o = sb("gain_o", [P, GV])
        wg = sb("wg", [RANK + 1, GH * GK])
        pscale = sb("pscale", [P, 2])
        cnt = sb("cnt", [P, TS])
        pat = sb("pat", [P, TS], U32)
        cand = sb("cand", [P, TS], U32)
        undo = sb("undo", [P, TS], U32)
        ahead = sb("ahead", [P, TS], U32)
        bits = sb("bits", [P, 2, TS], U32)
        need = sb("need", [P, TS])
        gss = sb("gss", [P, 2, GH])
        grs = sb("grs", [P, GH])
        gdec = sb("gdec", [P, 4])
        dec = sb("dec", [P, 2, 4])
        mx = sb("mx", [P, 3])
        nmx = sb("nmx", [P, 3])
        rsum = sb("rsum", [P, PAIRS, T, 2])
        rinv = sb("rinv", [P, PAIRS, T, 2])
        ssq = sb("ssq", [P, 32])
        rqk = sb("rqk", [P, 32])

        kib = 1024
        placed = {}

        def place(items):
            with ExitStack() as layer:
                at = 0
                for name, shape, dt, first in sorted(items, key=lambda x: x[3]):
                    assert first >= at, (name, first, at)
                    if first > at:
                        layer.enter_context(nc.sbuf_tensor(f"gap_{name}", [P, first - at], U8))
                    placed[name] = layer.enter_context(nc.sbuf_tensor(name, shape, dt))
                    size = int(np.prod(shape[1:])) * {F32: 4, F32R: 4, BF16: 2, U8: 1}[dt]
                    at = first + (size + 31) // 32 * 32
                    placed.setdefault("top", 0)
                    placed["top"] = max(placed["top"], at)

        SC, RL, EV, GL = 124 * kib, 141 * kib, 150 * kib, 156 * kib
        place([("hT_hi", [P, K, S], F32R, 0), ("hT_lo", [P, K, S], F32R, 32 * kib),
               ("w_hi", [P, 2, K, WB], F32R, 64 * kib), ("w_lo", [P, 2, K, WB], F32R, 88 * kib),
               ("w_raw", [P, K, WB], F32, 112 * kib),
               ("scores", [P, SOFF[T]], F32, SC), ("relus", [P, 2, S], F32, RL),
               ("evac", [P, 4, WB], F32, EV),
               ("stage", [P, 2, 6, P], F32, GL), ("iqT", [P, IH, TS * P], F32R, GL + 6 * kib),
               ("ikT", [P, 2, S], F32R, GL + 18 * kib)])
        g = GL
        gla = []
        for name, shape, dt in (
                ("gin", [P, 2, CW], F32), ("ggs", [P, RANK], F32), ("ggT", [RANK + 1, P], F32), ("nl", [P, GH, GP], F32),
                ("sp_a", [P, GH, GK], F32), ("sp_r", [P, GH, GK], F32), ("eb", [P, GH, GK], F32),
                ("enb", [P, GH, GK], F32), ("ed", [P, GH, GK], F32), ("qs", [P, GH, GP], F32),
                ("ks", [P, GH, GP], F32), ("kd", [P, GH, GP], F32), ("qkT", [P, 2, 4, P], F32),
                ("kv", [P, 2, 2, 2, GV], F32), ("state", [P, 5, 2, GV], F32),
                ("att", [P, GH, P], F32), ("osb", [P, 2, GH, GV], F32), ("osq", [P, GH, GV], F32),
                ("yT", [P, 3, P], F32)):
            gla.append((name, shape, dt, g))
            g += int(np.prod(shape[1:])) * 4
        place(gla)
        place([("xT_raw", [P, 4, S], F32, SC), ("x_sum", [P, 2, S], F32, RL), ("x_sq", [P, K, S], F32, GL)])
        place([("uT", [P, 2, PADL + S], F32, SC), ("zT", [P, 2, S], F32, SC + 8320),
               ("win", [P, 2, PADL + S], F32, RL)])
        place([("rdiag", [P, T, P], F32, RL), ("rstdB", [P, S], F32, EV), ("wpd", [P, 2, P], F32, EV + 4 * kib)])
        place([("wo_hi", [P, K, 512], F32R, 0), ("wo_lo", [P, K, 512], F32R, 16 * kib),
               ("wo_raw", [P, 4, 512], F32, 32 * kib), ("mixA", [P, PAIRS, S], F32, 40 * kib),
               ("kT", [P, 2, 2, S], F32R, 56 * kib), ("v", [P, T, PAIRS * P], F32, 72 * kib),
               ("qT", [P, 2, S], F32R, 88 * kib), ("prob", [P, 3, S], F32, 96 * kib),
               ("oT_a", [P, S], F32, 108 * kib), ("gate", [P, T, PAIRS * P], F32, 112 * kib),
               ("mix_raw", [P, K - PAIRS, S], F32, 124 * kib), ("oT_b", [P, S], F32, 144 * kib),
               ("probT", [P, 2, T, P], F32, 148 * kib),
               ("raw_qk", [P, 2, T, P], F32, GL), ("sq", [P, 2, T, P], F32, GL + 8 * kib),
               ("qk_st", [P, 2, 2, T, P], F32, GL + 16 * kib)])
        place([("mix_hi", [P, K, S], F32R, 52 * kib), ("mix_lo", [P, K, S], F32R, 84 * kib),
               ("res", [P, 4, 512], F32, 116 * kib), ("outb", [P, 4, 512], F32, 148 * kib),
               ("wo_hi2", [P, K, 512], F32R, GL), ("wo_lo2", [P, K, 512], F32R, GL + 16 * kib)])
        v_ = placed
        hT_hi, hT_lo, w_hi, w_lo, w_raw = (v_[n] for n in ("hT_hi", "hT_lo", "w_hi", "w_lo", "w_raw"))
        scores, relus, evac, stage, iqT, ikT = (v_[n] for n in ("scores", "relus", "evac", "stage", "iqT", "ikT"))
        (gin, ggs, ggT, nl, sp_a, sp_r, eb, enb, ed, qs, ks, kd, qkT, kv, state, att, osb, osq, yT) = (
            v_[n[0]] for n in gla)
        xT_raw, x_sum, x_sq, uT, zT, win, rdiag, rstdB, wpd = (
            v_[n] for n in ("xT_raw", "x_sum", "x_sq", "uT", "zT", "win", "rdiag", "rstdB", "wpd"))
        (wo_hi, wo_lo, wo_raw, mixA, qT, kT, prob, probT, v, gate, raw_qk, sq, qk_st, mix_hi, mix_lo, res,
         outb, mix_raw, wo_hi2, wo_lo2) = (v_[n] for n in (
             "wo_hi", "wo_lo", "wo_raw", "mixA", "qT", "kT", "prob", "probT", "v", "gate", "raw_qk", "sq",
             "qk_st", "mix_hi", "mix_lo", "res", "outb", "mix_raw", "wo_hi2", "wo_lo2"))
        oT = [v_["oT_a"], v_["oT_b"]]
        relu_flat = relus[:, :, :].rearrange("p a n -> p (a n)")
        seen = relu_flat.bitcast(U8)
        whole = ctx.enter_context(nc.sbuf_tensor("region", [P, v_["top"]], U8))
        del whole

        pA = ctx.enter_context(nc.psum_tensor("pA", [P, 2, 512], F32))
        pB = ctx.enter_context(nc.psum_tensor("pB", [P, 2, 512], F32))
        p4, p5, p6, p7 = (ctx.enter_context(nc.psum_tensor(f"p{i}", [P, 512], F32)) for i in range(4, 8))
        bank = [pA[:, 0, :], pA[:, 1, :], pB[:, 0, :], pB[:, 1, :], p4[:, :], p5[:, :], p6[:, :], p7[:, :]]

        proj_c = nc.dram_tensor("proj_c", [S, CW], F32).ap()
        proj_a = nc.dram_tensor("proj_a", [S, AW], F32).ap()
        pool_d = nc.dram_tensor("pool_d", [2, P, S], F32).ap()
        gla_d = nc.dram_tensor("gla_d", [3, P, P + S], F32).ap()

        const_in = sem("const_in")
        xT_in = [sem(f"xT_in{i}") for i in range(4)]
        w_in = [sem(f"w_in{k}") for k in range(K)]
        hT_ready, w_ready = sem("hT_ready"), sem("w_ready")
        x_squared, last_added, x_summed, ss_made, ms_ready, rstd_ready = (
            sem(n) for n in ("x_squared", "last_added", "x_summed", "ss_made", "ms_ready", "rstd_ready"))
        idx_made, idx_staged, idx_turned, idx_kept = (
            sem("idx_made"), sem("idx_staged"), sem("idx_turned"), sem("idx_kept"))
        dots_made, dots_relu, dots_added = sem("dots_made"), sem("dots_relu"), sem("dots_added")
        proj_made, proj_kept = sem("proj_made"), sem("proj_kept")
        spilled = [sem(f"spilled{i}") for i in range(4)]
        mask_ready = sem("mask_ready")
        dve_done, act_done, pool_done = sem("dve_done"), sem("act_done"), sem("pool_done")
        gin_in = [sem(f"gin_in{i}") for i in range(2)]
        ggs_ready = sem("ggs_ready")
        ggT_made, z_made, sums_made, qkT_made, att_made, o_made, y_turned = (
            sem(n) for n in ("ggT_made", "z_made", "sums_made", "qkT_made", "att_made", "o_made", "y_turned"))
        ggT_kept, sp_kept, exps_kept, qkT_kept, att_kept, o_kept, y_kept = (
            sem(n) for n in ("ggT_kept", "sp_kept", "exps_kept", "qkT_kept", "att_kept", "o_kept", "y_kept"))
        nl_done, scaled_done, state_done, masked_done, y_done = (
            sem(n) for n in ("nl_done", "scaled_done", "state_done", "masked_done", "y_done"))
        kv_kept, y_out, gla_clear = sem("kv_kept"), sem("y_out"), sem("gla_clear")
        rdiag_ready, rstdB_made, rstdB_ready = sem("rdiag_ready"), sem("rstdB_made"), sem("rstdB_ready")
        wpd_clear, wpd_in = sem("wpd_clear"), sem("wpd_in")
        pf_made, pf_kept, silu_done = sem("pf_made"), sem("pf_kept"), sem("silu_done")
        pooled_done, yb_made, yb_done, yb_out = sem("pooled_done"), sem("yb_made"), sem("yb_done"), sem("yb_out")
        qk_in, v_in, z_in = sem("qk_in"), sem("v_in"), sem("z_in")
        qk_squared, qk_summed, qk_split = sem("qk_squared"), sem("qk_summed"), sem("qk_split")
        qk_normed, sums_inverted = sem("qk_normed"), sem("sums_inverted")
        turned, kept_act, kept_dve, swapped = sem("turned"), sem("kept_act"), sem("kept_dve"), [sem(f"swapped{i}") for i in range(2)]
        logits_made, logits_read, max_ready, prob_done = (
            sem(n) for n in ("logits_made", "logits_read", "max_ready", "prob_done"))
        pv_made, pv_kept, gate_silu, gate_done, mixA_done = (
            sem(n) for n in ("pv_made", "pv_kept", "gate_silu", "gate_done", "mixA_done"))
        passed = sem("passed")
        wo_in = [sem(f"wo_in{i}") for i in range(4)]
        wo_ready = sem("wo_ready")
        mix_in = sem("mix_in")
        mixhi_ready, mixlo_ready, out_made, out_added = (
            sem("mixhi_ready"), sem("mixlo_ready"), sem("out_made"), sem("out_added"))
        res_in = [sem(f"res_in{i}") for i in range(4)]
        out_out = [sem(f"out_out{i}") for i in range(4)]

        block = ctx.enter_context(nc.Block())
        SMALL = 8 * 16
        NU = NC_UNITS + 4 * T
        NDOT = TS * IH
        NBK = NU // 4 * 16
        OUT_ORDER = [3, 4, 5, 6, 7, 0, 1, 2]
        OUT_TILES = [0, 1, 2, 3, 6, 4, 5, 7]
        BEFORE_TURN = [(0, 0), (0, 2), (2, 4), (4, 6), (6, 8), (8, 8), (8, 8), (8, 8)]
        OUT_EARLY = {HEADS * T - 1: 1, HEADS * T + 1: 3}
        YB_BANK = [1, 3, 6, 7]

        def flat(ap):
            return ap.rearrange("p a n -> p (a n)")

        def tiles(t0, n=1):
            return slice(t0 * P, (t0 + n) * P)

        def idx_kept_after(t):
            return t + 1 if t < T0 else T0 + 2 * (t + 1 - T0)

        def groups(t):
            return [range(a, min(a + 4, t + 1)) for a in range(0, t + 1, 4)]

        STEPS = HEADS * T

        def tile_of(s):
            return s % T if s // T < HEADS - 1 else T - 1 - s % T

        QK_ROUND = 12
        head_group, prob_group, gate_group, plan = {}, {}, {}, []
        group_no = 0
        for i in range(-1, STEPS + 4):
            todo = []
            if i == -1:
                todo += [("head", (0, n)) for n in range(4)]
            elif i // T + 1 < HEADS and 3 <= i % T < 7:
                todo.append(("head", (i // T + 1, i % T - 3)))
            if i > 3 and (i - 3) % (2 * T) == 0:
                todo += [("gate", ((i - 3) // (2 * T) - 1, n)) for n in range(2)]
            if 2 <= i < STEPS + 2:
                todo += [("prob", (i - 2, tuple(grp))) for grp in groups(tile_of(i - 2))]
            for kind, what in todo:
                {"head": head_group, "prob": prob_group, "gate": gate_group}[kind][what] = group_no + todo.index((kind, what))
            plan.append([(group_no + n, kind, what) for n, (kind, what) in enumerate(todo)])
            group_no += len(todo)
        by_act = [False] * group_no
        for todo in plan:
            for no, kind, what in todo:
                by_act[no] = kind == "prob" and what[1][0] == 0 or kind == "head" and what[1] % 2 == 1

        def wait_kept(engine, no):
            engine.wait_ge(kept_act if by_act[no] else kept_dve, sum(a == by_act[no] for a in by_act[:no + 1]))

        def group_bank(no):
            return bank[(4, 5, 7)[no % 3]]

        def last_prob_group(s):
            return max(no for (step, _), no in prob_group.items() if step == s)

        def times_gate(ops, p):
            g = gate[:, :, p * P:(p + 1) * P].rearrange("p t (h n) -> p t h n", h=2)
            ops.tensor_tensor(g, g, rinv[:, p, :, :, None].broadcast_to([P, T, 2, HD]), ALU.mult).then_inc(gate_done, 1)

        def alone(engine):
            engine.sem_inc(passed, 1)

        @block.sync
        def _(sp):
            def load_w(n_at, width, k):
                return sp.dma_start(w_raw[:, k, 0:width], d["w"][k * P:(k + 1) * P, n_at:n_at + width])

            sp.dma_start(norm_g[:, :], d["norm_g"]).then_inc(const_in, 16)
            for k in range(K):
                if k >= 4:
                    sp.wait_ge(hT_ready, k - 3)
                    sp.wait_ge(x_squared, k - 3)
                sp.dma_start(xT_raw[:, k % 4, :], d["xT"][k * P:(k + 1) * P, :]).then_inc(xT_in[k % 4], 16)
                load_w(0, BLOCK_W[0], k).then_inc(w_in[k], 16)
            for name, dst in (("const", const[:, :]), ("qgain", qgain[:, :]), ("kgain", kgain[:, :]),
                              ("gain_o", gain_o[:, :]), ("pscale", pscale[:, :]),
                              ("w_gate", wg[0:RANK, :]), ("b_gate", wg[RANK:RANK + 1, :])):
                sp.dma_start(dst, d[name]).then_inc(const_in, 16)
            for t in range(T):
                sp.wait_ge(w_ready, t + 1)
                load_w(BLOCK_AT[1], WB, t).then_inc(w_in[t], 16)
            for k in range(K):
                sp.wait_ge(w_ready, K + k + 1)
                load_w(BLOCK_AT[2], WB, k).then_inc(w_in[k], 16)
            for n in range(1, 4):
                for t in range(T):
                    u = (n - 1) * T + t
                    sp.wait_ge(proj_kept, u + 1)
                    sp.dma_start(proj_c[tiles(t), (n - 1) * WB:n * WB], evac[:, u % 4, :]).then_inc(spilled[u % 4], 16)
                    sp.wait_ge(w_ready, K * (n + 1) + t + 1)
                    load_w(BLOCK_AT[n + 2], WB, t).then_inc(w_in[t], 16)
            for i in range(4):
                sp.wait_ge(spilled[i], NC_UNITS // 4 * 16)
            with sp.Fori(0, 2) as it:
                for b in range(2):
                    blk = it * 2 + b
                    for j in range(2):
                        sp.wait_ge(y_done, it * 4 + (2 * b + j) + 1)
                        sp.dma_start(gin[:, j, :], proj_c[bass.ds((blk * 2 + j) * P, P), :]).then_inc(gin_in[j], 16)
                    for t in range(T):
                        sp.wait_ge(proj_kept, it * 16 + (NC_UNITS + 8 * b + t + 1))
                        sp.dma_start(proj_a[tiles(t), bass.ds(blk * WB, WB)], evac[:, t % 4, :]).then_inc(spilled[t % 4], 16)
                        sp.wait_ge(w_ready, it * 16 + (K * (5 + b) + t + 1))
                        sp.dma_start(w_raw[:, t, :], d["w"][t * P:(t + 1) * P, bass.ds(blk * WB + (A0 + 2 * WB), WB)]).then_inc(w_in[t], 16)
                        if t in (0, 7):
                            j = t // 7
                            sp.wait_ge(y_kept, it * 4 + (2 * b + j + 2))
                            alone(sp)
                            sp.dma_start(gla_d[:, :, bass.ds((blk * 2 + j) * P, P)].rearrange("c p n -> p c n"),
                                         yT[:, :, :]).then_inc(y_out, 16)
            for i in range(4):
                sp.wait_ge(spilled[i], NBK)
            sp.wait_ge(y_done, T + 2)
            for w in range(2):
                sp.dma_start(raw_qk[:, w, :, :], proj_a[:, w * WB:w * WB + P].rearrange("(t p) n -> p t n", p=P)).then_inc(qk_in, 16)
            sp.wait_ge(y_kept, T + 2)
            sp.dma_start(gla_d[:, :, S:S + P].rearrange("c p n -> p c n"), yT[:, :, :]).then_inc(y_out, 16)
            sp.wait_ge(wpd_clear, 1)
            for grp in range(4):
                o = HD * (grp % 2)
                sp.dma_start(wpd[o:o + HD, grp // 2, o:o + HD], d["pool_w"][grp]).then_inc(wpd_in, 16)

            def load_qk(p):
                for w in range(2):
                    sp.dma_start(raw_qk[:, w, :, :], proj_a[:, w * WB + p * P:w * WB + p * P + P].rearrange("(t p) n -> p t n", p=P)).then_inc(qk_in, 16)

            sp.wait_ge(w_ready, NBLK * K)
            sp.dma_start(gate[:, :, :], proj_a[:, 3 * WB:4 * WB].rearrange("(t p) n -> p t n", p=P)).then_inc(z_in, 16)
            sp.wait_ge(qk_normed, 1)
            load_qk(1)

            def load_wo(n):
                k, half = n % K, n // K
                if n >= 4:
                    sp.wait_ge(wo_ready, n - 3)
                sp.dma_start(wo_raw[:, n % 4, :], d["w_out"][OUT_ORDER[k] * P:(OUT_ORDER[k] + 1) * P,
                                                            512 * half:512 * half + 512]).then_inc(wo_in[n % 4], 16)

            def swap(h):
                for half in range(2):
                    wait_kept(sp, head_group[h, 1 + 2 * half])
                    cols = slice(512 * half, 512 * half + 512)
                    for a, b in ((0, HD), (HD, 0)):
                        sp.dma_start(kT[a:a + HD, h % 2, 1, cols].bitcast(F32), kT[b:b + HD, h % 2, 0, cols].bitcast(F32)).then_inc(swapped[half], 16)

            swap(0)
            sp.wait_ge(pf_made, 8)
            sp.dma_start(v[:, :, :], proj_a[:, 2 * WB:3 * WB].rearrange("(t p) n -> p t n", p=P)).then_inc(v_in, 16)
            for n in range(4):
                load_wo(n)
            for u in range(4):
                sp.wait_ge(yb_done, u + 1)
                sp.dma_start(pool_d[u // 2, :, 512 * (u % 2):512 * (u % 2) + 512], zT[:, u // 2, 512 * (u % 2):512 * (u % 2) + 512]).then_inc(yb_out, 16)
            swap(1)
            sp.wait_ge(qk_normed, 2)
            load_qk(2)
            for n in range(4, 8):
                load_wo(n)
            for h in range(2, HEADS):
                swap(h)
                if h == 2:
                    sp.wait_ge(yb_out, 4 * 16)
                    sp.wait_ge(y_out, (T + 2) * 16)
                    for n in range(K - PAIRS):
                        sp.dma_start(mix_raw[:, n, :], pool_d[n] if n < 2 else gla_d[n - 2, :, P:]).then_inc(mix_in, 16)
                if h == 3:
                    for n in range(8, 12):
                        load_wo(n)
            for n in range(12, 16):
                load_wo(n)
            sp.wait_ge(turned, group_no)
            def out_at(u):
                return (tiles(OUT_TILES[u]), slice(0, 512)) if u < T else (tiles(u - T), slice(512, 1024))

            for u in range(4):
                sp.dma_start(res[:, u, :], d["x"][out_at(u)]).then_inc(res_in[u], 16)
            for u in range(2 * T):
                sp.wait_ge(out_added, u + 1)
                sp.dma_start(d["out"][out_at(u)], outb[:, u % 4, :]).then_inc(out_out[u % 4], 16)
                if u + 4 < 2 * T:
                    sp.dma_start(res[:, u % 4, :], d["x"][out_at(u + 4)]).then_inc(res_in[u % 4], 16)
            for i in range(4):
                sp.wait_ge(out_out[i], 4 * 16)

        @block.tensor
        def _(pe):
            def project(out, t, buf, width, first_k=0, last_k=K, ready=None):
                for k in range(first_k, last_k):
                    if ready is not None:
                        pe.wait_ge(w_ready, ready + k + 1)
                    for n, (a, w) in enumerate(((hT_hi, w_hi), (hT_hi, w_lo), (hT_lo, w_hi))):
                        last = nc.tensor.matmul(out, a[:, k, tiles(t)], w[:, buf, k, 0:width],
                                                start=(k == 0 and n == 0), stop=(k == K - 1 and n == 2))
                return last

            passes = ((hT_hi, w_hi), (hT_hi, w_lo), (hT_lo, w_hi))
            pe.wait_ge(dve_done, 1)
            pe.wait_ge(pool_done, 2)
            for n, (a, w) in enumerate(passes):
                if n == 1:
                    pe.wait_ge(w_ready, 1)
                if n == 2:
                    pe.wait_ge(hT_ready, 1)
                for t in range(T - 2):
                    nc.tensor.matmul(bank[t][:, 0:IDXW], a[:, 0, tiles(t)], w[:, 0, 0, 0:IDXW], start=(n == 0), stop=False)
            for k in range(1, K):
                pe.wait_ge(hT_ready, k + 1)
                pe.wait_ge(w_ready, k + 1)
                for t in range(T - 2):
                    last = project(bank[t][:, 0:IDXW], t, 0, IDXW, k, k + 1)
                    if k == K - 1:
                        last.then_inc(idx_made, 1)

            def piece(n):
                t, k = T - 2 + n // K, n % K
                last = project(bank[t][:, 0:IDXW], t, 0, IDXW, k, k + 1)
                if k == K - 1:
                    last.then_inc(idx_made, 1)

            for n in range(0):
                piece(n)
            pe.wait_ge(const_in, SMALL)
            pe.wait_ge(x_summed, 1)
            for t in range(T):
                last = nc.tensor.matmul(bank[T - 1][:, t:t + 1], x_sum[:, 0, tiles(t)], ones[:, 0:1], start=True, stop=True)
            last.then_inc(ss_made, 1)
            for n in range(0, K):
                piece(n)
            pe.wait_ge(ms_ready, 1)
            for t in range(T):
                for n in range(*BEFORE_TURN[t]):
                    piece(K + n)
                pe.wait_ge(idx_staged, t + 1)
                if t >= T0:
                    for h in range(IH):
                        nc.tensor.transpose(bank[t][:, h * P:(h + 1) * P], stage[:, t % 2, h, :], ident)
                    pe.wait_ge(idx_kept, idx_kept_after(t - T0))
                for m in range(2):
                    last = nc.tensor.transpose(bank[t if t < T0 else t - T0][:, m * P:(m + 1) * P], stage[:, t % 2, 4 + m, :], ident)
                last.then_inc(idx_turned, 1)
            pe.wait_ge(idx_kept, idx_kept_after(T - 1))

            def dots(n):
                t, h = T0 + n // IH, n % IH
                width = (t + 1) * P
                if n >= 2:
                    pe.wait_ge(dots_relu, n - 1)
                dst = (pA, pB)[n % 2]
                for c in range(0, width, 512):
                    w = min(512, width - c)
                    for m in range(2):
                        last = nc.tensor.matmul(dst[:, c // 512, 0:w], iqT[:, h, (t - T0) * P:(t - T0 + 1) * P],
                                                ikT[:, m, c:c + w], start=(m == 0), stop=(m == 1))
                last.then_inc(dots_made, 1)

            for n in range(1, 4):
                for t in range(T):
                    u = (n - 1) * T + t
                    if n == 1 and t < TS:
                        for h in range(IH):
                            dots(t * IH + h)
                    if u >= 2:
                        pe.wait_ge(proj_kept, u - 1)
                    project(bank[4 + u % 2][:, 0:WB], t, n % 2, WB, ready=n * K if t == 0 else None).then_inc(proj_made, 1)

            pe.wait_ge(dots_relu, NDOT)
            pe.wait_ge(gla_clear, 1)

            def gla(stage_no, i, j, rounds):
                if stage_no == 1:
                    if j == 0:
                        pe.wait_ge(y_kept, i + 1)
                    pe.wait_ge(ggs_ready, i + 1)
                    nc.tensor.transpose(bank[0][0:RANK, 0:P], ggs[:, :], ident).then_inc(ggT_made, 1)
                if stage_no == 2:
                    pe.wait_ge(ggT_kept, i + 1)
                    nc.tensor.matmul(bank[1][:, 0:GH * GK], ggT[:, :], wg[:, :], start=True, stop=True).then_inc(z_made, 1)
                if stage_no == 3:
                    pe.wait_ge(nl_done, i + 1)
                    if j == 0:
                        pe.wait_ge(ggT_kept, i + 2)
                    nc.tensor.matmul(bank[2][:, 0:GH * GK], tri_upto, nl[:, :, 0:GK], start=True, stop=True)
                    nc.tensor.matmul(bank[2][:, 256:256 + GH * GK], tri_after, nl[:, :, 0:GK], start=True, stop=True)
                    for p in range(2):
                        last = nc.tensor.matmul(bank[0][:, 2 * p:2 * p + 2], flat(nl[:, 2 * p:2 * p + 2, :]), in_chunk,
                                                start=True, stop=True)
                    last.then_inc(sums_made, 1)
                if stage_no == 4:
                    pe.wait_ge(scaled_done, i + 1)
                    pe.wait_ge(gin_in[j], rounds * 16 + 16)
                    if j == 1:
                        pe.wait_ge(kv_kept, i)
                    for n, src in enumerate((qs, ks)):
                        for p in range(2):
                            nc.tensor.transpose(bank[3][:, (2 * n + p) * P:(2 * n + p + 1) * P], flat(src[:, 2 * p:2 * p + 2, :]), ident)
                    for c in range(2):
                        rows = slice(CH * c, CH * c + CH)
                        for h in range(GH):
                            p, hh = h // 2, h % 2
                            last = nc.tensor.matmul(bank[6 + c][GP * hh:GP * hh + GP, GV * p:GV * p + GV], kd[rows, h, :],
                                                    gin[rows, j, WB + GV * h:WB + GV * h + GV], start=True, stop=True)
                    last.then_inc(qkT_made, 1)
                if stage_no == 5:
                    pe.wait_ge(qkT_kept, i + 1)
                    if j == 0:
                        pe.wait_ge(exps_kept, i + 2)
                    for h in (0, 2, 1, 3):
                        p, hh = h // 2, h % 2
                        rows = slice(GP * hh, GP * hh + GK)
                        last = nc.tensor.matmul(bank[2 - hh][:, p * P:(p + 1) * P], qkT[rows, j, 2 + p, :], qkT[rows, j, p, :],
                                                start=True, stop=True)
                    last.then_inc(att_made, 1)
                if stage_no == 6:
                    pe.wait_ge(masked_done, i + 1)
                    pe.wait_ge(state_done, i + 1)
                    if j == 0:
                        pe.wait_ge(kv_kept, i + 2)
                    for h in (0, 2, 1, 3):
                        p, hh = h // 2, h % 2
                        rows = slice(GP * hh, GP * hh + GK)
                        cols = slice(GV * p, GV * p + GV)
                        o_bank = bank[3 * (1 + hh)]
                        nc.tensor.matmul(o_bank[:, cols], att[:, h, :], gin[:, j, WB + GV * h:WB + GV * h + GV],
                                         start=True, stop=False, skip_group_check=True)
                        for c in range(2):
                            last = nc.tensor.matmul(o_bank[CH * c:CH * c + CH, cols], qkT[rows, j, p, CH * c:CH * c + CH],
                                                    state[rows, 2 * j + c, p, :], start=False, stop=(c == 1), skip_group_check=True)
                    last.then_inc(o_made, 1)
                if stage_no == 7:
                    pe.wait_ge(y_done, i + 3)
                    for c in range(3):
                        last = nc.tensor.transpose(bank[3 * j][:, c * P:(c + 1) * P], flat(osb[:, j, :, :])[:, c * P:(c + 1) * P], ident)
                    last.then_inc(y_turned, 1)

            with pe.Fori(0, 2) as it:
                for b in range(2):
                    for t in range(T):
                        pe.wait_ge(proj_kept, it * 16 + (NC_UNITS + 8 * b + t - 1))
                        project(bank[4 + t % 2][:, 0:WB], t, b, WB, ready=it * 16 + K * (4 + b) if t == 0 else None).then_inc(proj_made, 1)
                        if t == 0:
                            gla(7, it * 4 + (2 * b - 1), 1, None)
                        if t < 6:
                            gla(t + 1, it * 4 + 2 * b, 0, it * 2 + b)
                        if 0 < t < 7:
                            gla(t, it * 4 + (2 * b + 1), 1, it * 2 + b)
                        if t == 7:
                            gla(7, it * 4 + 2 * b, 0, None)

            for u in range(8):
                m, half = u // 2, u % 2
                if u == 2:
                    gla(7, T - 1, 1, None)
                if u == 1:
                    pe.wait_ge(rdiag_ready, 1)
                    pe.wait_ge(y_kept, T + 1)
                    for c in range(2):
                        last = nc.tensor.matmul(pA[:, c, :], ones, flat(rdiag[:, 4 * c:4 * c + 4, :]), start=True, stop=True)
                    last.then_inc(rstdB_made, 1)
                if u == 6:
                    pe.wait_ge(w_ready, 10 * K)
                if u < 2:
                    pe.wait_ge(proj_kept, NU)
                else:
                    pe.wait_ge(pf_kept, u - 1)
                buf, col = (0, m * P) if m < 3 else (1, 0)
                for k in range(K):
                    if u == 0:
                        pe.wait_ge(w_ready, 8 * K + k + 1)
                    for n, (w, a) in enumerate(((w_hi, hT_hi), (w_hi, hT_lo), (w_lo, hT_hi))):
                        last = nc.tensor.matmul(bank[4 + u % 2], w[:, buf, k, col:col + P], a[:, k, 512 * half:512 * half + 512],
                                                start=(k == 0 and n == 0), stop=(k == K - 1 and n == 2))
                last.then_inc(pf_made, 1)

            def turn(no, kind, what):
                if no >= 3:
                    wait_kept(pe, no - 3)
                if kind == "head":
                    (h, n), w = what, what[1] % 2
                    sources = [qk_st[:, w, h % 2, 4 * (n // 2) + i, :] for i in range(4)]
                    if n == 0:
                        pe.wait_ge(qk_split, h + 1)
                elif kind == "prob":
                    sources = [prob[:, what[0] % 3, kt * P:(kt + 1) * P] for kt in what[1]]
                    pe.wait_ge(prob_done, what[0] + 1)
                else:
                    p, n = what
                    sources = [gate[:, 4 * n + i, p * P:(p + 1) * P] for i in range(4)]
                    pe.wait_ge(gate_done, p + 1)
                for n, src in enumerate(sources):
                    last = nc.tensor.transpose(group_bank(no)[:, n * P:(n + 1) * P], src, ident)
                last.then_inc(turned, 1)

            def logits(s):
                h, t = s // T, tile_of(s)
                if s >= 2:
                    pe.wait_ge(logits_read, s - 1)
                for half in range(2):
                    if s % T != (4 * half if h < HEADS - 1 else 0):
                        continue
                    wait_kept(pe, head_group[h, 2 * half])
                    wait_kept(pe, head_group[h, 2 * half + 1])
                    pe.wait_ge(swapped[half], 32 * (h + 1))
                width = (t + 1) * P
                dst = (pA, pB)[s % 2]
                for c in range(0, width, 512):
                    w = min(512, width - c)
                    for m in range(2):
                        last = nc.tensor.matmul(dst[:, c // 512, 0:w], qT[:, h % 2, tiles(t)], kT[:, h % 2, m, c:c + w],
                                                start=(m == 0), stop=(m == 1))
                last.then_inc(logits_made, 1)

            def pv(s):
                h, t = s // T, tile_of(s)
                if s == 0:
                    pe.wait_ge(v_in, 16)
                if s >= 1:
                    pe.wait_ge(pv_kept, s)
                for grp in groups(t):
                    wait_kept(pe, prob_group[s, tuple(grp)])
                rows = slice(HD * (h % 2), HD * (h % 2) + HD)
                for kt in range(t + 1):
                    last = nc.tensor.matmul(bank[6][rows, 0:P], v[:, kt, HD * h:HD * h + HD],
                                            probT[:, s % 2, kt, :], start=(kt == 0), stop=(kt == t))
                last.then_inc(pv_made, 1)

            pe.wait_ge(pf_kept, 8)
            for group in plan[0]:
                turn(*group)
            pe.wait_ge(wpd_in, 4 * 16)
            for u in range(4):
                m, half = u // 2, u % 2
                pe.wait_ge(pooled_done, m + 1)
                if u == 3:
                    wait_kept(pe, 2)
                nc.tensor.matmul(bank[YB_BANK[u]], wpd[:, m, :], uT[:, m, PADL + 512 * half:PADL + 512 * half + 512],
                                 start=True, stop=True).then_inc(yb_made, 1)
            def out(t, k, w_hi_, w_lo_):
                for n, (a, w) in enumerate(((mix_hi, w_hi_), (mix_hi, w_lo_), (mix_lo, w_hi_))):
                    last = nc.tensor.matmul(bank[t], a[:, k, tiles(t)], w[:, k, :],
                                            start=(k == 0 and n == 0), stop=(k == K - 1 and n == 2))
                return last

            for i in range(STEPS + 3):
                if i == 2:
                    pe.wait_ge(yb_done, 4)
                if i < STEPS:
                    logits(i)
                for group in plan[i + 1]:
                    turn(*group)
                if i >= 3:
                    pv(i - 3)
                if i in OUT_EARLY:
                    pe.wait_ge(wo_ready, 1)
                    pe.wait_ge(mixhi_ready, 1)
                    pe.wait_ge(mixlo_ready, 1)
                    pe.wait_ge(logits_read, STEPS - 4)
                    out(OUT_EARLY[i], 0, wo_hi, wo_lo)

            for k in range(K):
                pe.wait_ge(wo_ready, k + 1)
                pe.wait_ge(mixhi_ready, k + 1)
                pe.wait_ge(mixlo_ready, k + 1)
                for t in OUT_TILES:
                    if k == 0 and t in OUT_EARLY.values():
                        continue
                    if k == 0 and t == 0:
                        pe.wait_ge(logits_read, STEPS)
                    if k == 0 and t == 6:
                        for group in plan[STEPS + 4]:
                            turn(*group)
                        pe.wait_ge(pv_kept, STEPS)
                    if k == 0 and t in (4, 5, 7):
                        for no in range(group_no - 3, group_no):
                            if (4, 5, 7)[no % 3] == t:
                                wait_kept(pe, no)
                    last = out(t, k, wo_hi, wo_lo)
                    if k == K - 1:
                        last.then_inc(out_made, 1)
            for t in range(T):
                if t == 0:
                    pe.wait_ge(wo_ready, 2 * K)
                pe.wait_ge(out_added, OUT_TILES.index(t) + 1)
                for k in range(K):
                    last = out(t, k, wo_hi2, wo_lo2)
                last.then_inc(out_made, 1)

        @block.scalar
        def _(act):
            own = Chain(act, act_done)

            for k in range(K):
                act.wait_ge(xT_in[k % 4], 16 * (k // 4 + 1))
                nc.scalar.activation(x_sq[:, k, :], xT_raw[:, k % 4, :], ACT.Square).then_inc(x_squared, 1)
            for s, n in ((y_kept, 1), (y_out, 16)):
                act.sem_inc(s, n)
            for t in range(T):
                act.wait_ge(idx_turned, t + 1)
                if t >= T0:
                    nc.scalar.activation(iqT[:, :, (t - T0) * P:(t - T0 + 1) * P],
                                         bank[t].rearrange("p (h n) -> p h n", h=IH), ACT.Copy).then_inc(idx_kept, 1)
                nc.scalar.activation(ikT[:, :, tiles(t)],
                                     bank[t if t < T0 else t - T0][:, 0:2 * P].rearrange("p (m n) -> p m n", m=2),
                                     ACT.Copy).then_inc(idx_kept, 1)

            def relu(n):
                t = T0 + n // IH
                act.wait_ge(dots_made, n + 1)
                if n >= 2:
                    act.wait_ge(dots_added, n - 1)
                src = flat((pA, pB)[n % 2][:, :, :])
                nc.scalar.activation(relus[:, n % 2, 0:(t + 1) * P], src[:, 0:(t + 1) * P], ACT.Relu).then_inc(dots_relu, 1)

            def keep(u_off, u, t, func, spills):
                act.wait_ge(proj_made, u_off + (u + 1))
                if spills is not None:
                    act.wait_ge(spilled[u % 4], spills)
                nc.scalar.activation(evac[:, u % 4, :], bank[4 + u % 2][:, 0:WB], func,
                                     scale=rstd[:, t:t + 1]).then_inc(proj_kept, 1)

            for n in range(1, 4):
                for t in range(T):
                    u = (n - 1) * T + t
                    if n == 1 and t < TS:
                        for h in range(IH):
                            relu(t * IH + h)
                    keep(0, u, t, ACT.Silu if n == 3 else ACT.Copy, 16 * (u // 4) if u >= 4 else None)
            act.wait_ge(gla_clear, 1)

            def turn_in(i, tile_at):
                nc.scalar.activation(ggs[:, :], gg[:, bass.ds(tile_at, 1), :].rearrange("p a n -> p (a n)"), ACT.Copy).then_inc(ggs_ready, 1)

            def gla(stage_no, i, j):
                if stage_no == 1:
                    act.wait_ge(ggT_made, i + 1)
                    nc.scalar.activation(ggT[0:RANK, :], bank[0][0:RANK, 0:P], ACT.Copy).then_inc(ggT_kept, 1)
                if stage_no == 2:
                    act.wait_ge(z_made, i + 1)
                    z = bank[1][:, 0:GH * GK].rearrange("p (h n) -> p h n", h=GH)
                    nc.scalar.activation(sp_r[:, :, :], z, ACT.Relu, scale=-1.0)
                    own.link(nc.scalar.activation(sp_a[:, :, :], z, ACT.Abs))
                    own.link(nc.scalar.activation(sp_a[:, :, :], sp_a[:, :, :], ACT.Exp, scale=-1.0))
                    nc.scalar.activation(sp_a[:, :, :], sp_a[:, :, :], ACT.Ln, bias=1.0).then_inc(sp_kept, 1)
                if stage_no == 3:
                    act.wait_ge(sums_made, i + 1)
                    upto = bank[2][:, 0:GH * GK].rearrange("p (h n) -> p h n", h=GH)
                    after = bank[2][:, 256:256 + GH * GK].rearrange("p (h n) -> p h n", h=GH)
                    nc.scalar.activation(eb[:, :, :], upto, ACT.Exp, scale=-1.0 / TAU)
                    nc.scalar.activation(enb[:, :, :], upto, ACT.Exp, scale=1.0 / TAU)
                    nc.scalar.activation(ed[:, :, :], after, ACT.Exp, scale=-1.0 / TAU)
                    nc.scalar.activation(gdec[:, :], bank[0][:, 0:4], ACT.Exp, scale=-1.0 / TAU).then_inc(exps_kept, 1)
                if stage_no == 4:
                    act.wait_ge(qkT_made, i + 1)
                    src = bank[3].rearrange("p (a n) -> p a n", a=4)
                    nc.scalar.activation(qkT[:, j, 0:2, :], src[:, 0:2, :], ACT.Copy, scale=float(GK) ** -0.5)
                    nc.scalar.activation(qkT[:, j, 2:4, :], src[:, 2:4, :], ACT.Copy).then_inc(qkT_kept, 1)
                    for c in range(2):
                        last = nc.scalar.activation(flat(kv[:, j, c, :, :]), bank[6 + c][:, 0:2 * GV], ACT.Copy)
                    last.then_inc(kv_kept, 1)
                if stage_no == 5:
                    act.wait_ge(att_made, i + 1)
                    for hh in range(2):
                        dst = att[:, :, :].rearrange("p (a b) n -> p b a n", b=2)[:, hh]
                        src = bank[2 - hh][:, 0:2 * P].rearrange("p (a n) -> p a n", a=2)
                        for c in range(2):
                            r = slice(CH * c, CH * c + CH)
                            last = nc.scalar.activation(dst[r, :, r], src[r, :, r], ACT.Copy)
                    last.then_inc(att_kept, 1)
                if stage_no == 6:
                    act.wait_ge(o_made, i + 1)
                    for h in range(GH):
                        nc.scalar.activation(osq[:, h, :], bank[3 * (1 + h % 2)][:, GV * (h // 2):GV * (h // 2) + GV], ACT.Square,
                                             accum_out=gss[:, j, h:h + 1])
                    for hh in range(2):
                        last = nc.scalar.activation(osb[:, j, :, :].rearrange("p (a b) n -> p b a n", b=2)[:, hh],
                                                    bank[3 * (1 + hh)][:, 0:2 * GV].rearrange("p (a n) -> p a n", a=2), ACT.Copy)
                    last.then_inc(o_kept, 1)
                if stage_no == 7:
                    act.wait_ge(y_turned, i + 2)
                    act.wait_ge(y_out, i * 16 + 32)
                    nc.scalar.activation(flat(yT[:, :, :]), bank[3 * j][:, 0:3 * P], ACT.Copy).then_inc(y_kept, 1)

            with act.Fori(0, 2) as it:
                own.loop(it, 2 * 2 * 2)
                for b in range(2):
                    for t in range(T):
                        if t < 2:
                            if t == 1:
                                act.wait_ge(ggT_made, it * 4 + (2 * b + 1))
                            turn_in(None, it * 4 + (2 * b + t))
                        act_u = NC_UNITS + 8 * b + t
                        keep(it * 16, act_u, t, ACT.Copy, it * 64 + 16 * (act_u // 4))
                        if t == 0:
                            gla(7, it * 4 + (2 * b - 1), 1)
                        if t < 6:
                            gla(t + 1, it * 4 + 2 * b, 0)
                        if 0 < t < 7:
                            gla(t, it * 4 + (2 * b + 1), 1)
                        if t == 7:
                            gla(7, it * 4 + 2 * b, 0)
                own.end(2)

            for i in range(4):
                act.wait_ge(spilled[i], NBK)
            act.wait_ge(rstdB_made, 1)
            nc.scalar.activation(rstdB[:, :], flat(pA[:, :, :]), ACT.Copy).then_inc(rstdB_ready, 1)

            def squares(p, w):
                act.wait_ge(qk_in, p * 32 + 32)
                nc.scalar.activation(flat(sq[:, w, :, :]), flat(raw_qk[:, w, :, :]), ACT.Square).then_inc(qk_squared, 1)

            def mix_high(k):
                c = OUT_ORDER[k]
                if c >= PAIRS:
                    act.wait_ge(mix_in, 16 * (K - PAIRS))
                if k == 1:
                    act.wait_ge(pv_made, STEPS)
                if c < PAIRS:
                    act.wait_ge(mixA_done, c + 1)
                src = mix_raw[:, k, :] if c >= PAIRS else mixA[:, c, :]
                nc.scalar.activation(mix_hi[:, k, :], src, ACT.Copy).then_inc(mixhi_ready, 1)

            squares(0, 0)
            squares(0, 1)
            gla(7, T - 1, 1)
            for u in range(4, 8):
                act.wait_ge(pf_kept, u + 1)
                z = zT[:, (u - 4) // 2, 512 * (u % 2):512 * (u % 2) + 512]
                nc.scalar.activation(z, z, ACT.Silu).then_inc(silu_done, 1)
                if u == 4:
                    act.wait_ge(qk_split, 2)
                    squares(1, 0)
                    squares(1, 1)

            def keep_groups(i):
                for no, kind, what in plan[i + 1]:
                    if by_act[no]:
                        act.wait_ge(turned, no + 1)
                        if kind == "head":
                            (h, n) = what
                            dst = (kT[:, h % 2, 0, :] if n % 2 else qT[:, h % 2, :])[:, 512 * (n // 2):512 * (n // 2) + 512]
                        else:
                            s, grp = what
                            dst = flat(probT[:, s % 2, grp[0]:grp[-1] + 1, :])
                            if s >= 2:
                                act.wait_ge(pv_made, s - 1)
                        nc.scalar.activation(dst, group_bank(no)[:, 0:dst.shape[-1]], ACT.Copy).then_inc(kept_act, 1)

            keep_groups(-1)
            act.wait_ge(z_in, 16)
            nc.scalar.activation(flat(gate[:, :, :]), flat(gate[:, :, :]), ACT.Silu).then_inc(gate_silu, 1)
            for i in range(STEPS + 4):
                if i >= 4:
                    s = i - 4
                    h, t = s // T, tile_of(s)
                    act.wait_ge(pv_made, s + 1)
                    if h >= 4:
                        act.wait_ge(mixA_done, h // 2 - 1)
                    rows = slice(HD * (h % 2), HD * (h % 2) + HD)
                    nc.scalar.activation(oT[(h // 2) % 2][rows, tiles(t)], bank[6][rows, 0:P], ACT.Copy).then_inc(pv_kept, 1)
                if i < STEPS + 3:
                    keep_groups(i)
                if i < STEPS:
                    h, t = i // T, tile_of(i)
                    act.wait_ge(max_ready, i + 1)
                    nc.scalar.activation(prob[:, i % 3, 0:(t + 1) * P], prob[:, i % 3, 0:(t + 1) * P], ACT.Exp,
                                         bias=nmx[:, i % 3:i % 3 + 1], accum_out=rsum[:, h // 2, t, h % 2:h % 2 + 1]).then_inc(prob_done, 1)
                if i in (QK_ROUND, QK_ROUND + 1):
                    act.wait_ge(qk_split, 4)
                    squares(2, i - QK_ROUND)
                if i == STEPS - 10:
                    mix_high(0)

            for k in range(1, K):
                mix_high(k)

        @block.vector
        def _(dve):
            own = Chain(dve, dve_done)
            link = own.link
            vec = nc.vector
            dve.wait_ge(const_in, 16)
            for k in range(K):
                dve.wait_ge(xT_in[k % 4], 16 * (k // 4 + 1))
                link(vec.tensor_scalar(hT_hi[:, k, :], xT_raw[:, k % 4, :], norm_g[:, k:k + 1], None, ALU.mult))
                vec.scalar_tensor_tensor(out=hT_lo[:, k, :], in0=xT_raw[:, k % 4, :], scalar=norm_g[:, k:k + 1],
                                         in1=hT_hi[:, k, :].bitcast(F32), op0=ALU.mult, op1=ALU.subtract).then_inc(hT_ready, 1)
            dve.wait_ge(x_squared, K - 2)
            link(vec.tensor_tensor(x_sum[:, 0, :], x_sq[:, 0, :], x_sq[:, 1, :], ALU.add))
            for k in range(2, K - 2):
                link(vec.tensor_tensor(x_sum[:, 0, :], x_sum[:, 0, :], x_sq[:, k, :], ALU.add))
            dve.wait_ge(last_added, 1)
            vec.tensor_tensor(x_sum[:, 0, :], x_sum[:, 0, :], x_sum[:, 1, :], ALU.add).then_inc(x_summed, 1)
            dve.wait_ge(ss_made, 1)
            vec.tensor_scalar(rtmp[:, 0:T], bank[T - 1][:, 0:T], 1.0 / D, EPS, ALU.mult, ALU.add).then_inc(ms_ready, 1)
            dve.sem_inc(y_done, 2)
            dve.wait_ge(rstd_ready, 1)
            def stage_high(t):
                dve.wait_ge(idx_made, t + 1)
                if t >= 2:
                    dve.wait_ge(idx_turned, t - 1)
                own.step(vec.tensor_scalar(stage[:, t % 2, 0:5, 0:IDIM].bitcast(F32R), bank[t][:, 0:5 * IDIM].rearrange("p (h n) -> p h n", h=5),
                                           rstd[:, t:t + 1], None, ALU.mult))

            stage_high(0)
            for t in range(T):
                r = rstd[:, t:t + 1]
                src = bank[t][:, 0:5 * IDIM].rearrange("p (h n) -> p h n", h=5)
                st = stage[:, t % 2, :, :]
                own.wait()
                own.step(vec.scalar_tensor_tensor(out=st[:, 0:5, IDIM:P], in0=src, scalar=r, in1=st[:, 0:5, 0:IDIM],
                                                  op0=ALU.mult, op1=ALU.subtract))
                vec.tensor_scalar(gg[:, t, :], bank[t][:, IDXW - RANK:IDXW], r, None, ALU.mult)
                vec.tensor_scalar(iw[:, t, :], bank[t][:, 5 * IDIM:5 * IDIM + IH], r, IH ** -0.5, ALU.mult, ALU.mult)
                vec.tensor_copy(st[:, 5, IDIM:P], st[:, 4, 0:IDIM])
                own.wait()
                vec.tensor_copy(st[:, 5, 0:IDIM], st[:, 4, IDIM:P]).then_inc(idx_staged, 1)
                if t + 1 < T:
                    stage_high(t + 1)
            for n in range(NDOT):
                t, h = T0 + n // IH, n % IH
                sc = scores[:, SOFF[t]:SOFF[t + 1]]
                wgt = iw[:, t, h:h + 1]
                dve.wait_ge(dots_relu, n + 1)
                if h == 0:
                    vec.tensor_scalar(sc, relus[:, n % 2, 0:(t + 1) * P], wgt, None, ALU.mult).then_inc(dots_added, 1)
                else:
                    dve.wait_ge(dots_added, n)
                    vec.scalar_tensor_tensor(out=sc, in0=relus[:, n % 2, 0:(t + 1) * P], scalar=wgt, in1=sc,
                                             op0=ALU.mult, op1=ALU.add).then_inc(dots_added, 1)
                if h == IH - 1:
                    dve.wait_ge(dots_added, n + 1)
                    diag = scores[:, SOFF[t] + t * P:SOFF[t + 1]]
                    own.step(vec.tensor_tensor(diag, diag, causal, ALU.add))
            own.wait()

            def count(thresholds, op, dst):
                link(count_tiles(thresholds, op, dst, T0, T))

            def count_tiles(thresholds, op, dst, first, end):
                for t in range(first, end):
                    at = thresholds if isinstance(thresholds, float) else thresholds[:, t - T0:t - T0 + 1]
                    last = vec.tensor_scalar(out=seen[:, SOFF[t]:SOFF[t + 1]], in0=scores[:, SOFF[t]:SOFF[t + 1]], scalar1=at,
                                             scalar2=None, op0=op, op1=ALU.add, accum_out=dst[:, t - T0:t - T0 + 1])
                return last

            own.step(vec.memset(bits[:, 0, :], 1 << 30))
            count(0.0, ALU.is_ge, cnt)
            link(vec.tensor_scalar(pat[:, :], cnt[:, :], float(TOPK), None, ALU.is_lt))
            link(vec.tensor_scalar(pat[:, :].bitcast(I32), pat[:, :].bitcast(I32), 31, 31, ALU.arith_shift_left, ALU.arith_shift_right))
            link(vec.tensor_tensor(cand[:, :], pat[:, :], bits[:, 0, :], ALU.bitwise_xor))

            def try_bit(n):
                bit, below = bits[:, n, :], bits[:, 1 - n, :]
                own.step(vec.tensor_scalar(below, bit, 1, None, ALU.logical_shift_right))
                count_tiles(cand[:, :].bitcast(F32), ALU.is_ge, cnt, T0, T - 2)
                own.wait()
                vec.tensor_tensor(ahead[:, :], cand[:, :], below, ALU.bitwise_xor)
                link(count_tiles(cand[:, :].bitcast(F32), ALU.is_ge, cnt, T - 2, T))
                link(vec.scalar_tensor_tensor(out=undo[:, :], in0=cnt[:, :], scalar=float(TOPK), in1=bit, op0=ALU.is_lt, op1=ALU.mult))
                link(vec.tensor_tensor(cand[:, :], ahead[:, :], undo[:, :], ALU.bitwise_xor))

            with dve.Fori(0, 15) as i:
                own.loop(i, 8)
                try_bit(0)
                try_bit(1)
                own.end(15)
            try_bit(0)
            thr = cand[:, :].bitcast(F32)
            count(thr, ALU.is_gt, cnt)
            link(vec.tensor_scalar(need[:, :], cnt[:, :], -1.0, float(TOPK), ALU.mult, ALU.add))
            for t in range(T0, T):
                sc, m = scores[:, SOFF[t]:SOFF[t + 1]], mask[:, MOFF[t]:MOFF[t + 1]]
                width, at = (t + 1) * P, slice(t - T0, t - T0 + 1)
                eq, upto = relus[:, 0, 0:width], relus[:, 1, 0:width]
                link(vec.tensor_scalar(eq, sc, thr[:, at], None, ALU.is_equal))
                link(vec.tensor_tensor_scan(out=upto, data0=eq, data1=eq, initial=0.0, op0=ALU.add, op1=ALU.max))
                link(vec.scalar_tensor_tensor(out=eq, in0=upto, scalar=need[:, at], in1=eq, op0=ALU.is_le, op1=ALU.mult))
                link(vec.scalar_tensor_tensor(out=upto, in0=sc, scalar=thr[:, at], in1=eq, op0=ALU.is_gt, op1=ALU.add))
                link(vec.tensor_scalar(m, upto, -NEGM, NEGM, ALU.mult, ALU.add))
            link(vec.memset(mask[:, MOFF[1]:MOFF[1] + P], 0.0))
            for t in range(T0):
                vec.tensor_copy(mask[:, MOFF[t] + t * P:MOFF[t + 1]], causal)
            for t in range(T):
                last = vec.tensor_scalar(rdiag[:, t, :], ident, rstd[:, t:t + 1], None, ALU.mult)
            link(last)
            dve.sem_inc(rdiag_ready, 1)

            vec.memset(uT[:, :, 0:PADL], 0.0)
            dve.wait_ge(rstdB_made, 1)
            link(vec.memset(win[:, :, 0:PADL], 0.0))
            dve.wait_ge(rstdB_ready, 1)

            def keep(u):
                dve.wait_ge(pf_made, u + 1)
                m, half = u // 2, u % 2
                cols = slice(512 * half, 512 * half + 512)
                dst = uT[:, m, PADL + 512 * half:PADL + 512 * half + 512] if m < 2 else zT[:, m - 2, cols]
                vec.tensor_tensor(dst, bank[4 + u % 2], rstdB[:, cols], ALU.mult).then_inc(pf_kept, 1)

            def add_shifted(dst, src, shift, rows):
                link(vec.tensor_tensor(dst[rows, shift:PADL + S], src[rows, shift:PADL + S], src[rows, 0:PADL + S - shift], ALU.add))

            def pool(m):
                dve.wait_ge(pf_kept, 2 * m + 2)
                a, b, u_ = win[:, 0, :], win[:, 1, :], uT[:, m, :]
                both, low, high = slice(0, P), slice(0, HD), slice(HD, P)
                add_shifted(a, u_, 1, both)
                if m == 0:
                    add_shifted(b, a, 2, high)
                else:
                    add_shifted(b, a, 2, both)
                    add_shifted(a, b, 4, both)
                    add_shifted(b, a, 8, high)
                for r, w in ((low, a), (high, b)):
                    head, rest = slice(PADL, 2 * PADL), slice(2 * PADL, PADL + S)
                    link(vec.tensor_tensor(w[r, head], w[r, head], pool_cnt[r, m, :], ALU.mult))
                    own.step(vec.tensor_tensor(u_[r, head], w[r, head], u_[r, head], ALU.subtract))
                    link(vec.scalar_tensor_tensor(out=u_[r, rest], in0=w[r, rest], scalar=pool_w1[r, m:m + 1], in1=u_[r, rest],
                                                  op0=ALU.mult, op1=ALU.subtract))
                dve.sem_inc(pooled_done, 1)

            def sums(p, w):
                dve.wait_ge(qk_squared, 2 * p + w + 1)
                vec.tensor_reduce(ssq[:, 2 * T * w:2 * T * (w + 1)], sq[:, w, :, :].rearrange("p t (h n) -> p (t h) n", h=2), axis=AX.X,
                                  op=ALU.add).then_inc(qk_summed, 1)

            keep(0)
            sums(0, 0)
            sums(0, 1)
            for u in range(1, 4):
                keep(u)
            pool(0)
            for u in range(4, 6):
                keep(u)
            pool(1)
            for u in range(6, 8):
                keep(u)

            def keep_groups(i):
                for no, kind, what in plan[i + 1]:
                    if by_act[no]:
                        continue
                    dve.wait_ge(turned, no + 1)
                    if kind == "gate":
                        p, n = what
                        cols = slice(512 * n, 512 * n + 512)
                        dve.wait_ge(pv_kept, (p + 1) * 2 * T)
                        vec.tensor_tensor(mixA[:, p, cols], group_bank(no), oT[p % 2][:, cols], ALU.mult).then_inc(kept_dve, 1)
                        if n == 1:
                            wait_kept(dve, no)
                            dve.sem_inc(mixA_done, 1)
                        continue
                    if kind == "head":
                        (h, n) = what
                        dst = (kT[:, h % 2, 0, :] if n % 2 else qT[:, h % 2, :])[:, 512 * (n // 2):512 * (n // 2) + 512]
                    else:
                        s, grp = what
                        dst = flat(probT[:, s % 2, grp[0]:grp[-1] + 1, :])
                        if s >= 2:
                            dve.wait_ge(pv_made, s - 1)
                    vec.tensor_copy(dst, group_bank(no)[:, 0:dst.shape[-1]]).then_inc(kept_dve, 1)

            keep_groups(-1)
            sums(1, 0)
            sums(1, 1)
            for u in range(4):
                m, half = u // 2, u % 2
                dve.wait_ge(yb_made, u + 1)
                dve.wait_ge(silu_done, u + 1)
                z = zT[:, m, 512 * half:512 * half + 512]
                vec.scalar_tensor_tensor(out=z, in0=bank[YB_BANK[u]], scalar=pscale[:, m:m + 1], in1=z, op0=ALU.mult, op1=ALU.mult).then_inc(yb_done, 1)

            def mix_low(k):
                c = OUT_ORDER[k]
                dve.wait_ge(mixhi_ready, k + 1)
                src = mix_raw[:, k, :] if c >= PAIRS else mixA[:, c, :]
                vec.tensor_tensor(mix_lo[:, k, :], src, mix_hi[:, k, :].bitcast(F32), ALU.subtract).then_inc(mixlo_ready, 1)

            for i in range(STEPS + 4):
                if i < STEPS:
                    t = tile_of(i)
                    width = (t + 1) * P
                    dve.wait_ge(logits_made, i + 1)
                    if i >= 3:
                        dve.wait_ge(turned, last_prob_group(i - 3) + 1)
                    vec.tensor_tensor_reduce(out=prob[:, i % 3, 0:width], in0=flat((pA, pB)[i % 2][:, :, :])[:, 0:width],
                                             in1=mask[:, MOFF[t]:MOFF[t + 1]], scale=1.0, scalar=NEG, op0=ALU.add, op1=ALU.max,
                                             accum_out=mx[:, i % 3:i % 3 + 1]).then_inc(logits_read, 1)
                    dve.wait_ge(logits_read, i + 1)
                    vec.tensor_scalar(nmx[:, i % 3:i % 3 + 1], mx[:, i % 3:i % 3 + 1], -1.0, None, ALU.mult).then_inc(max_ready, 1)
                if i % (2 * T) == 1 and i > 1:
                    p = i // (2 * T) - 1
                    dve.wait_ge(prob_done, (p + 1) * 2 * T)
                    link(vec.reciprocal(flat(rinv[:, p, :, :]), flat(rsum[:, p, :, :])))
                    dve.sem_inc(sums_inverted, 1)
                    if p != 1:
                        times_gate(vec, p)
                keep_groups(i)
                if i - 1 in (QK_ROUND, QK_ROUND + 1):
                    sums(2, i - 1 - QK_ROUND)
                if i == STEPS - 9:
                    mix_low(0)

            for k in range(1, K):
                mix_low(k)
            for u in range(2 * T):
                dve.wait_ge(out_made, u + 1)
                dve.wait_ge(res_in[u % 4], 16 * (u // 4 + 1))
                if u >= 4:
                    dve.wait_ge(out_out[u % 4], 16 * (u // 4))
                vec.tensor_tensor(outb[:, u % 4, :], bank[OUT_TILES[u] if u < T else u - T], res[:, u % 4, :], ALU.add).then_inc(out_added, 1)

        @block.gpsimd
        def _(pool):
            own = Chain(pool, pool_done, alone)
            link = own.link
            gp = nc.gpsimd

            def split_w(buf, k, width, arrived):
                pool.wait_ge(w_in[k], arrived)
                if not isinstance(arrived, int):
                    alone(pool)
                link(gp.tensor_scalar(w_hi[:, buf, k, 0:width], w_raw[:, k, 0:width], 1.0, 1.0, ALU.mult, ALU.mult))
                gp.tensor_tensor(w_lo[:, buf, k, 0:width], w_raw[:, k, 0:width], w_hi[:, buf, k, 0:width].bitcast(F32),
                                 ALU.subtract).then_inc(w_ready, 1)

            own.step(gp.memset(neghalf[:, :], -0.5))
            for n in range(5):
                if n == 1:
                    pool.wait_ge(x_squared, K)
                    gp.tensor_tensor(x_sum[:, 1, :], x_sq[:, K - 2, :], x_sq[:, K - 1, :], ALU.add).then_inc(last_added, 1)
                    pool.wait_ge(ms_ready, 1)
                    gp.tensor_tensor(rstd[:, :], rtmp[:, 0:T], neghalf[:, 0:T], ALU.pow).then_inc(rstd_ready, 1)
                if n == 2:
                    pool.wait_ge(idx_made, T)
                if n > 2:
                    pool.wait_ge(proj_made, T * (n - 2))
                for k in range(K):
                    split_w(n % 2, k, BLOCK_W[n], 16 * (n + 1))

            pool.wait_ge(dots_made, NDOT)
            for buf, val in ((nl, 0.0), (qs, 0.0), (ks, 0.0), (kd, 0.0), (att, 0.0)):
                gp.memset(buf[:, :, :], val)
            gp.memset(osb[:, 1, :, :], 0.0)
            gp.memset(state[:, 4, :, :], 0.0)
            link(gp.memset(ggT[:, :], 1.0))
            pool.sem_inc(gla_clear, 1)

            def gla(stage_no, i, j, rounds):
                if stage_no == 2:
                    pool.wait_ge(sp_kept, i + 1)
                    gp.tensor_tensor(nl[:, :, 0:GK], sp_a[:, :, :], sp_r[:, :, :], ALU.add).then_inc(nl_done, 1)
                if stage_no == 3:
                    pool.wait_ge(exps_kept, i + 1)
                    pool.wait_ge(gin_in[j], rounds * 16 + 16)
                    q = gin[:, j, 0:GH * GK].rearrange("p (h n) -> p h n", h=GH)
                    k = gin[:, j, GH * GK:2 * GH * GK].rearrange("p (h n) -> p h n", h=GH)
                    gp.tensor_tensor(qs[:, :, 0:GK], q, eb[:, :, :], ALU.mult)
                    gp.tensor_tensor(ks[:, :, 0:GK], k, enb[:, :, :], ALU.mult)
                    gp.tensor_tensor(kd[:, :, 0:GK], k, ed[:, :, :], ALU.mult)
                    gp.tensor_scalar(dec[:, j, :], gdec[:, :], 1.0, 1.0, ALU.mult, ALU.mult).then_inc(scaled_done, 1)
                if stage_no == 4:
                    pool.wait_ge(kv_kept, i + 1)
                    pool.wait_ge(scaled_done, i + 1)
                    alone(pool)
                    if j == 0:
                        link(gp.tensor_scalar(flat(state[:, 0, :, :]), flat(state[:, 4, :, :]), 1.0, 1.0, ALU.mult, ALU.mult))
                    for c in range(2):
                        n = 2 * j + c
                        for p in range(2):
                            own.step(gp.tensor_scalar(state[:, n + 1, p, :], state[:, n, p, :], dec[:, j, 2 * p + c:2 * p + c + 1], 1.0, ALU.mult, ALU.mult))
                        own.wait()
                        own.step(gp.tensor_tensor(flat(state[:, n + 1, :, :]), flat(state[:, n + 1, :, :]), flat(kv[:, j, c, :, :]), ALU.add))
                        own.wait()
                    pool.sem_inc(state_done, 1)
                if stage_no == 5:
                    pool.wait_ge(att_kept, i + 1)
                    alone(pool)
                    gp.affine_select(out=att[:, :, :], in_=att[:, :, :], compare_op=ALU.is_ge, fill=0.0, base=0,
                                     pattern=[[0, GH], [1, P]], channel_multiplier=-1).then_inc(masked_done, 1)
                if stage_no == 6:
                    pool.wait_ge(o_kept, i + 1)
                    alone(pool)
                    link(gp.tensor_scalar(grs[:, :], gss[:, j, :], 1.0 / GV, EPS, ALU.mult, ALU.add))
                    link(gp.tensor_tensor(grs[:, :], grs[:, :], neghalf[:, 0:GH], ALU.pow))
                    link(gp.tensor_tensor(osb[:, j, :, :], osb[:, j, :, :], grs[:, :, None].broadcast_to([P, GH, GV]), ALU.mult))
                    link(gp.tensor_tensor(osb[:, j, :, :], osb[:, j, :, :], gain_o[:, None, :].broadcast_to([P, GH, GV]), ALU.mult))
                    z = gin[:, j, 2 * WB:3 * WB]
                    gp.tensor_tensor(flat(osb[:, j, :, :]), flat(osb[:, j, :, :]), z, ALU.mult).then_inc(y_done, 1)

            with pool.Fori(0, 2) as it:
                own.loop(it, 2 * (K + 1 + 2 * 6 + 2 * 4))
                for b in range(2):
                    pool.wait_ge(proj_made, it * 16 + T * (3 + b))
                    for t in range(T):
                        split_w((b + 1) % 2, t, WB, it * 32 + 16 * (6 + b))
                        if t in (3, 5):
                            gla(t, it * 4 + (2 * b + 1), 1, it * 2 + b)
                        if t < 7:
                            gla(t + 1, it * 4 + 2 * b, 0, it * 2 + b)
                        if t > 0 and t not in (3, 5):
                            gla(t, it * 4 + (2 * b + 1), 1, it * 2 + b)
                own.end(2)
            for i in range(4):
                pool.wait_ge(spilled[i], NBK)
            link(gp.memset(wpd[:, :, :], 0.0))
            pool.sem_inc(wpd_clear, 1)
            pool.wait_ge(proj_made, T * 7)
            for k in range(K):
                split_w(1, k, BLOCK_W[9], 16 * 10)

            def norm_qk(p):
                pool.wait_ge(qk_in, p * 32 + 32)
                pool.wait_ge(qk_summed, 2 * p + 2)
                link(gp.tensor_scalar(rtmp[:, :], ssq[:, :], 1.0 / HD, EPS, ALU.mult, ALU.add))
                link(gp.tensor_tensor(rqk[:, :], rtmp[:, :], neghalf[:, :], ALU.pow))
                link(gp.tensor_scalar(rqk[:, 0:2 * T], rqk[:, 0:2 * T], HD ** -0.5, 1.0, ALU.mult, ALU.mult))
                for w in range(2):
                    raw = raw_qk[:, w, :, :].rearrange("p t (h n) -> p (t h) n", h=2)
                    nrm = sq[:, w, :, :].rearrange("p t (h n) -> p (t h) n", h=2)
                    link(gp.tensor_tensor(nrm, raw, rqk[:, 2 * T * w:2 * T * w + 2 * T, None].broadcast_to([P, 2 * T, HD]), ALU.mult))
                    own.step(gp.tensor_tensor(nrm, nrm, (qgain, kgain)[w][:, None, :].broadcast_to([P, 2 * T, HD]), ALU.mult))
                own.wait()
                pool.sem_inc(qk_normed, 1)

            def split_qk(h):
                if h == 0:
                    pool.wait_ge(y_turned, T + 1)
                if h >= 2:
                    pool.wait_ge(turned, head_group[h - 2, 3] + 1)
                for w in range(2):
                    st = qk_st[:, w, h % 2, :, :]
                    src = sq[:, w, :, HD * (h % 2):HD * (h % 2) + HD]
                    link(gp.tensor_scalar(st[:, :, 0:HD].bitcast(F32R), src, 1.0, 1.0, ALU.mult, ALU.mult))
                    last = gp.tensor_tensor(st[:, :, HD:P], src, st[:, :, 0:HD], ALU.subtract)
                last.then_inc(qk_split, 1)

            def split_wo(n, hi, lo):
                pool.wait_ge(wo_in[n % 4], 16 * (n // 4 + 1))
                k = n % K
                link(gp.tensor_scalar(hi[:, k, :], wo_raw[:, n % 4, :], 1.0, 1.0, ALU.mult, ALU.mult))
                gp.tensor_tensor(lo[:, k, :], wo_raw[:, n % 4, :], hi[:, k, :].bitcast(F32), ALU.subtract).then_inc(wo_ready, 1)

            def gate_of(p):
                pool.wait_ge(gate_silu, 1)
                pool.wait_ge(sums_inverted, p + 1)
                times_gate(gp, p)

            norm_qk(0)
            split_qk(0)
            split_qk(1)
            norm_qk(1)
            split_qk(2)
            split_qk(3)
            for n in range(4):
                split_wo(n, wo_hi, wo_lo)
            norm_qk(2)
            split_qk(4)
            for n in range(4, K):
                split_wo(n, wo_hi, wo_lo)
            split_qk(5)
            gate_of(1)
            pool.wait_ge(turned, head_group[HEADS - 1, 3] + 1)
            for n in range(K, 2 * K):
                split_wo(n, wo_hi2, wo_lo2)


def kernel(x, norm_g, w_in, att_q_gain, att_k_gain, pool_w, pool_scale, gla_w_gate, gla_b_gate,
           gla_out_gain, w_out):
    import concourse.bacc as bacc
    from concourse.bass_utils import run_bass_kernel_spmd as run

    def cols(a, b):
        return np.asarray(w_in)[0][:, a:b]

    def rows(a, n):
        return np.ascontiguousarray(np.broadcast_to(np.asarray(a).reshape(1, n), (P, n)))

    at = np.cumsum([0, 384, 384, 384, 384, 256, 64, 4, 256, 256, 192, 192, 384, 16, 384])
    aq, _, _, _, iq, _, iw, pu, _, gq, _, gv, gg, gz, end = at
    w = np.concatenate([cols(iq, pu), cols(gg, gz), cols(gq, gg), cols(gz, end), cols(aq, iq), cols(pu, gq),
                        np.zeros((D, WCOLS - B0 - BW), np.float32)], axis=1)
    j, i = np.arange(P)[:, None], np.arange(P)[None, :]
    same = (j // CH) == (i // CH)
    tok = np.arange(PADL)
    wins = [(2, 4), (8, 16)]
    cnt_ = np.zeros((P, 2, PADL), np.float32)
    w1 = np.zeros((P, 2), np.float32)
    for m in range(2):
        for g in range(2):
            cnt_[HD * g:HD * g + HD, m] = (1.0 / np.minimum(tok + 1, wins[m][g])).astype(np.float32)
            w1[HD * g:HD * g + HD, m] = 1.0 / wins[m][g]
    const = np.concatenate([
        np.eye(P), np.where(i <= j, 0.0, NEG), (j <= i) & same, (j > i) & same, np.ones((P, P)),
        j // CH == np.arange(2)[None, :], cnt_.reshape(P, 2 * PADL), w1], axis=1).astype(np.float32)
    assert const.shape == (P, CONSTS)
    x0 = np.ascontiguousarray(np.asarray(x)[0])
    arrays = {
        "x": x0, "xT": np.ascontiguousarray(x0.T),
        "norm_g": np.ascontiguousarray(np.asarray(norm_g)[0].reshape(K, P).T),
        "w": np.ascontiguousarray(w), "const": const,
        "qgain": rows(att_q_gain, HD), "kgain": rows(att_k_gain, HD), "gain_o": rows(gla_out_gain, GV),
        "pscale": np.ascontiguousarray(np.asarray(pool_scale)[0].reshape(2, P).T),
        "w_gate": np.ascontiguousarray(np.asarray(gla_w_gate)[0]),
        "b_gate": np.ascontiguousarray(np.asarray(gla_b_gate)[0].reshape(1, GH * GK)),
        "pool_w": np.ascontiguousarray(np.asarray(pool_w)[0]),
        "w_out": np.ascontiguousarray(np.asarray(w_out)[0]),
    }
    nc = bacc.Bacc("TRN2", target_bir_lowering=False, num_devices=1)
    d = {n: nc.dram_tensor(f"in_{n}", a.shape, F32, kind="ExternalInput").ap() for n, a in arrays.items()}
    d["out"] = nc.dram_tensor("out_dram", (S, D), F32, kind="ExternalOutput").ap()
    program(nc, d)
    r = run(nc, [{f"in_{n}": a for n, a in arrays.items()}], core_ids=[0])
    return r.results[0]["out_dram"].reshape(1, S, D)
```
